# Optimizing a Trainium2 kernel written in Bass

```python
import math
import jax, jax.numpy as jnp
from jax import lax
import numpy as np

D_MODEL = 2048
BATCH = 1
SEQ = 256
DEPTH = 1
DEC_BATCH = 8
DEC_SEQ = 1
PAST_LEN = 2048
PAGE_SIZE = 128

D_MIX = D_MODEL
W_LRU = D_MIX // 2
W_SSD = D_MIX - W_LRU
LRU_HEADS = 16
LRU_BLOCK = W_LRU // LRU_HEADS
LRU_C = 8.0
SSD_HEAD_DIM = 64
SSD_HEADS = W_SSD // SSD_HEAD_DIM
SSD_GROUPS = 2
SSD_HPG = SSD_HEADS // SSD_GROUPS
SSD_STATE = 128
SSD_CHUNK = 128
CONV_W = 4
SSD_CONV_DIM = W_SSD + 2 * SSD_GROUPS * SSD_STATE
IN_COLS = 2 * W_LRU + W_SSD + SSD_CONV_DIM + SSD_HEADS
D_FF = 5632
N_MOD = 9
EPS = 1e-6

kernel_name = "hymba_style_rglru_ssd_macaron_decoder_step"

def rmsnorm(x, g):
    xf = x.astype(jnp.float32)
    y = xf * lax.rsqrt(jnp.mean(xf * xf, axis=-1, keepdims=True) + EPS)
    return (y * g.astype(jnp.float32)).astype(x.dtype)

def modulate(h, shift, scale):
    return h * (1.0 + scale[:, None, :]) + shift[:, None, :]

def swiglu(h, w_up, w_down):
    g, u = jnp.split(h @ w_up, 2, axis=-1)
    return (jax.nn.silu(g) * u) @ w_down

def causal_conv(x, buf, w, b):
    T = x.shape[1]
    xp = jnp.concatenate([buf.astype(x.dtype), x], axis=1)
    y = b
    for k in range(CONV_W):
        y = y + w[k] * xp[:, k:k + T]
    return y, xp[:, xp.shape[1] - (CONV_W - 1):]

def rg_lru(x, h0, w_a, b_a, w_i, b_i, lam):
    Bsz, T, _ = x.shape
    xf = x.astype(jnp.float32)
    xb = xf.reshape(Bsz, T, LRU_HEADS, LRU_BLOCK)
    r = jax.nn.sigmoid(jnp.einsum('bthi,hij->bthj', xb, w_a).reshape(Bsz, T, W_LRU) + b_a)
    i = jax.nn.sigmoid(jnp.einsum('bthi,hij->bthj', xb, w_i).reshape(Bsz, T, W_LRU) + b_i)
    log_a = -LRU_C * r * jax.nn.softplus(-lam.astype(jnp.float32))
    a = jnp.exp(log_a)
    bt = jnp.sqrt(-jnp.expm1(2.0 * log_a)) * (i * xf)

    def combine(e1, e2):
        a1, b1 = e1
        a2, b2 = e2
        return a1 * a2, a2 * b1 + b2

    a_cum, b_cum = lax.associative_scan(combine, (a, bt), axis=1)
    h = a_cum * h0.astype(jnp.float32)[:, None, :] + b_cum
    return h, h[:, -1]

def ssd_scan(x, dt, A, Bm, Cm, h0):
    b, T = x.shape[0], x.shape[1]
    Lc = min(SSD_CHUNK, T)
    pad = (-T) % Lc
    if pad:
        padw = lambda t: jnp.pad(t, [(0, 0), (0, pad)] + [(0, 0)] * (t.ndim - 2))
        x, dt, Bm, Cm = padw(x), padw(dt), padw(Bm), padw(Cm)
    nc = (T + pad) // Lc
    G, E, P, N = SSD_GROUPS, SSD_HPG, SSD_HEAD_DIM, SSD_STATE
    x = x.reshape(b, nc, Lc, G, E, P)
    dt = dt.reshape(b, nc, Lc, G, E)
    Bm = Bm.reshape(b, nc, Lc, G, N)
    Cm = Cm.reshape(b, nc, Lc, G, N)
    dA_cs = jnp.cumsum(dt * A.reshape(G, E), axis=2)
    xdt = x * dt[..., None]
    diff = dA_cs[:, :, :, None] - dA_cs[:, :, None, :]
    causal = jnp.tril(jnp.ones((Lc, Lc), dtype=bool))[:, :, None, None]
    Lmat = jnp.exp(jnp.where(causal, diff, -jnp.inf))
    CB = jnp.einsum('bclgn,bcsgn->bclsg', Cm, Bm)
    M = CB[..., None] * Lmat
    y_diag = jnp.einsum('bclsge,bcsgep->bclgep', M, xdt)
    decay_last = jnp.exp(dA_cs[:, :, -1:] - dA_cs)
    states = jnp.einsum('bclgn,bclge,bclgep->bcgepn', Bm, decay_last, xdt)
    chunk_decay = jnp.exp(dA_cs[:, :, -1])

    def step(h, inp):
        s, d = inp
        return d[..., None, None] * h + s, h

    h_init = h0.astype(jnp.float32).reshape(b, G, E, P, N)
    hT, h_in = lax.scan(step, h_init, (jnp.moveaxis(states, 1, 0), jnp.moveaxis(chunk_decay, 1, 0)))
    h_in = jnp.moveaxis(h_in, 0, 1)
    y_off = jnp.einsum('bclgn,bcgepn,bclge->bclgep', Cm, h_in, jnp.exp(dA_cs))
    y = (y_diag + y_off).reshape(b, nc * Lc, SSD_HEADS, P)[:, :T]
    return y, hT.reshape(b, SSD_HEADS, P, N)

def hybrid_mixer(h, lru_h0, lru_buf0, ssm_h0, ssd_buf0, p):
    Bsz, T, _ = h.shape
    proj = h @ p['w_in']
    o1 = W_LRU
    o2 = o1 + W_LRU
    o3 = o2 + W_SSD
    o4 = o3 + SSD_CONV_DIM
    xl, gl, z, xbc, dt_raw = jnp.split(proj, [o1, o2, o3, o4], axis=-1)
    xl, lru_buf = causal_conv(xl, lru_buf0, p['lru_conv_w'], p['lru_conv_b'])
    hl, lru_hT = rg_lru(xl, lru_h0, p['lru_wa'], p['lru_ba'], p['lru_wi'], p['lru_bi'], p['lru_lambda'])
    out_l = hl * jax.nn.gelu(gl.astype(jnp.float32))
    xbc, ssd_buf = causal_conv(xbc, ssd_buf0, p['ssd_conv_w'], p['ssd_conv_b'])
    xbc = jax.nn.silu(xbc.astype(jnp.float32))
    xs, Bm, Cm = jnp.split(xbc, [W_SSD, W_SSD + SSD_GROUPS * SSD_STATE], axis=-1)
    dt = jax.nn.softplus(dt_raw.astype(jnp.float32) + p['ssd_dt_bias'].astype(jnp.float32))
    A = -jnp.exp(p['ssd_A_log'].astype(jnp.float32))
    xs4 = xs.reshape(Bsz, T, SSD_HEADS, SSD_HEAD_DIM)
    y, ssm_hT = ssd_scan(xs4, dt, A,
                         Bm.reshape(Bsz, T, SSD_GROUPS, SSD_STATE),
                         Cm.reshape(Bsz, T, SSD_GROUPS, SSD_STATE), ssm_h0)
    y = y + p['ssd_D'].astype(jnp.float32)[:, None] * xs4
    y = y.reshape(Bsz, T, W_SSD) * jax.nn.silu(z.astype(jnp.float32))
    y = rmsnorm(y, p['ssd_norm_g'])
    out = jnp.concatenate([out_l, y], axis=-1).astype(h.dtype) @ p['w_out']
    return out, (lru_hT, lru_buf, ssm_hT, ssd_buf)

def decoder_layer(x, c, lru_h0, lru_buf0, ssm_h0, ssd_buf0, p):
    mod = jax.nn.silu(c) @ p['w_ada'] + p['b_ada']
    sh1, sc1, g1, sh2, sc2, g2, sh3, sc3, g3 = jnp.split(mod, N_MOD, axis=-1)
    h = modulate(rmsnorm(x, p['g_ffn1']), sh1, sc1)
    x = x + 0.5 * g1[:, None, :] * swiglu(h, p['w_up1'], p['w_down1'])
    h = modulate(rmsnorm(x, p['g_mix']), sh2, sc2)
    o, new_state = hybrid_mixer(h, lru_h0, lru_buf0, ssm_h0, ssd_buf0, p)
    x = x + g2[:, None, :] * o
    h = modulate(rmsnorm(x, p['g_ffn2']), sh3, sc3)
    x = x + 0.5 * g3[:, None, :] * swiglu(h, p['w_up2'], p['w_down2'])
    return x, new_state

def setup_inputs(seed: int = 0) -> dict:
    key = jax.random.key(seed)
    ks = iter(jax.random.split(key, 48))
    f32 = jnp.float32
    nrm = lambda shape, s: jax.random.normal(next(ks), shape, f32) * s
    L = DEPTH
    u = jax.random.uniform(next(ks), (L, W_LRU), f32, 0.9, 0.999)
    a_base = u ** (1.0 / LRU_C)
    lru_lambda = jnp.log(a_base) - jnp.log1p(-a_base)
    dt0 = jnp.exp(jax.random.uniform(next(ks), (L, SSD_HEADS), f32, math.log(1e-3), math.log(1e-1)))
    ssd_dt_bias = dt0 + jnp.log(-jnp.expm1(-dt0))
    ssd_A_log = jnp.log(jax.random.uniform(next(ks), (L, SSD_HEADS), f32, 1.0, 16.0))
    return {
        'x_prompt': nrm((BATCH, SEQ, D_MODEL), 1.0),
        'x_sample': nrm((DEC_BATCH, DEC_SEQ, D_MODEL), 1.0),
        'c_prompt': nrm((BATCH, D_MODEL), 1.0),
        'c_sample': nrm((DEC_BATCH, D_MODEL), 1.0),
        'state_lru_h': nrm((L, DEC_BATCH, W_LRU), 0.5),
        'state_lru_conv': nrm((L, DEC_BATCH, CONV_W - 1, W_LRU), 1.0),
        'state_ssm': nrm((L, DEC_BATCH, SSD_HEADS, SSD_HEAD_DIM, SSD_STATE), 0.1),
        'state_ssd_conv': nrm((L, DEC_BATCH, CONV_W - 1, SSD_CONV_DIM), 1.0),
        'w_ada': nrm((L, D_MODEL, N_MOD * D_MODEL), 0.5 * D_MODEL ** -0.5),
        'b_ada': nrm((L, N_MOD * D_MODEL), 0.01),
        'g_ffn1': 1.0 + nrm((L, D_MODEL), 0.02),
        'w_up1': nrm((L, D_MODEL, 2 * D_FF), D_MODEL ** -0.5),
        'w_down1': nrm((L, D_FF, D_MODEL), D_FF ** -0.5),
        'g_mix': 1.0 + nrm((L, D_MODEL), 0.02),
        'w_in': nrm((L, D_MODEL, IN_COLS), D_MODEL ** -0.5),
        'lru_conv_w': nrm((L, CONV_W, W_LRU), CONV_W ** -0.5),
        'lru_conv_b': nrm((L, W_LRU), 0.01),
        'lru_wa': nrm((L, LRU_HEADS, LRU_BLOCK, LRU_BLOCK), LRU_BLOCK ** -0.5),
        'lru_ba': nrm((L, W_LRU), 0.01),
        'lru_wi': nrm((L, LRU_HEADS, LRU_BLOCK, LRU_BLOCK), LRU_BLOCK ** -0.5),
        'lru_bi': nrm((L, W_LRU), 0.01),
        'lru_lambda': lru_lambda,
        'ssd_conv_w': nrm((L, CONV_W, SSD_CONV_DIM), CONV_W ** -0.5),
        'ssd_conv_b': nrm((L, SSD_CONV_DIM), 0.01),
        'ssd_dt_bias': ssd_dt_bias,
        'ssd_A_log': ssd_A_log,
        'ssd_D': 1.0 + nrm((L, SSD_HEADS), 0.1),
        'ssd_norm_g': 1.0 + nrm((L, W_SSD), 0.02),
        'w_out': nrm((L, D_MIX, D_MODEL), D_MIX ** -0.5),
        'g_ffn2': 1.0 + nrm((L, D_MODEL), 0.02),
        'w_up2': nrm((L, D_MODEL, 2 * D_FF), D_MODEL ** -0.5),
        'w_down2': nrm((L, D_FF, D_MODEL), D_FF ** -0.5),
        'w_ada_f': nrm((D_MODEL, 2 * D_MODEL), 0.5 * D_MODEL ** -0.5),
        'b_ada_f': nrm((2 * D_MODEL,), 0.01),
        'g_final': 1.0 + nrm((D_MODEL,), 0.02),
    }

def reference(x_prompt, x_sample, c_prompt, c_sample, state_lru_h, state_lru_conv, state_ssm,
              state_ssd_conv, w_ada, b_ada, g_ffn1, w_up1, w_down1, g_mix, w_in, lru_conv_w,
              lru_conv_b, lru_wa, lru_ba, lru_wi, lru_bi, lru_lambda, ssd_conv_w, ssd_conv_b,
              ssd_dt_bias, ssd_A_log, ssd_D, ssd_norm_g, w_out, g_ffn2, w_up2, w_down2,
              w_ada_f, b_ada_f, g_final):
    xp, xs = x_prompt, x_sample
    bp = x_prompt.shape[0]
    dtp = x_prompt.dtype
    new_p = ([], [], [], [])
    new_s = ([], [], [], [])
    for l in range(DEPTH):
        p = {
            'w_ada': w_ada[l], 'b_ada': b_ada[l], 'g_ffn1': g_ffn1[l], 'w_up1': w_up1[l],
            'w_down1': w_down1[l], 'g_mix': g_mix[l], 'w_in': w_in[l],
            'lru_conv_w': lru_conv_w[l], 'lru_conv_b': lru_conv_b[l], 'lru_wa': lru_wa[l],
            'lru_ba': lru_ba[l], 'lru_wi': lru_wi[l], 'lru_bi': lru_bi[l],
            'lru_lambda': lru_lambda[l], 'ssd_conv_w': ssd_conv_w[l], 'ssd_conv_b': ssd_conv_b[l],
            'ssd_dt_bias': ssd_dt_bias[l], 'ssd_A_log': ssd_A_log[l], 'ssd_D': ssd_D[l],
            'ssd_norm_g': ssd_norm_g[l], 'w_out': w_out[l], 'g_ffn2': g_ffn2[l],
            'w_up2': w_up2[l], 'w_down2': w_down2[l],
        }
        xp, sp = decoder_layer(
            xp, c_prompt,
            jnp.zeros((bp, W_LRU), dtp),
            jnp.zeros((bp, CONV_W - 1, W_LRU), dtp),
            jnp.zeros((bp, SSD_HEADS, SSD_HEAD_DIM, SSD_STATE), dtp),
            jnp.zeros((bp, CONV_W - 1, SSD_CONV_DIM), dtp), p)
        xs, ss = decoder_layer(xs, c_sample, state_lru_h[l], state_lru_conv[l], state_ssm[l],
                               state_ssd_conv[l], p)
        for j in range(4):
            new_p[j].append(sp[j])
            new_s[j].append(ss[j])

    def final(x, c):
        shf, scf = jnp.split(jax.nn.silu(c) @ w_ada_f + b_ada_f, 2, axis=-1)
        return modulate(rmsnorm(x, g_final), shf, scf)

    y_prompt = final(xp, c_prompt).astype(x_prompt.dtype)
    y_sample = final(xs, c_sample).astype(x_sample.dtype)
    lru_h_prompt = jnp.stack(new_p[0]).astype(state_lru_h.dtype)
    lru_conv_prompt = jnp.stack(new_p[1]).astype(state_lru_conv.dtype)
    ssm_prompt = jnp.stack(new_p[2]).astype(state_ssm.dtype)
    ssd_conv_prompt = jnp.stack(new_p[3]).astype(state_ssd_conv.dtype)
    lru_h_sample = jnp.stack(new_s[0]).astype(state_lru_h.dtype)
    lru_conv_sample = jnp.stack(new_s[1]).astype(state_lru_conv.dtype)
    ssm_sample = jnp.stack(new_s[2]).astype(state_ssm.dtype)
    ssd_conv_sample = jnp.stack(new_s[3]).astype(state_ssd_conv.dtype)
    return (y_prompt, y_sample, lru_h_prompt, lru_conv_prompt, ssm_prompt, ssd_conv_prompt,
            lru_h_sample, lru_conv_sample, ssm_sample, ssd_conv_sample)


_drawn_inputs = setup_inputs


def setup_inputs(seed=0):
    import zlib

    import numpy as np

    out = dict(_drawn_inputs(seed))
    spreads = {}
    factors = {'g_ffn1': 8.0,
     'lru_ba': 34.135,
     'lru_bi': 8.0,
     'ssd_conv_b': 3.297,
     'ssd_D': 30.303,
     'ssd_norm_g': 64.0,
     'g_ffn2': 22.539,
     'b_ada_f': 4.318,
     'g_final': 8.594}
    for name, (base, spread) in spreads.items():
        noise = np.random.default_rng([zlib.crc32(name.encode()), seed]).standard_normal(out[name].shape)
        drawn = base * np.exp(spread * noise) if base else spread * noise
        out[name] = __import__('jax').numpy.asarray(drawn.astype(out[name].dtype))
    for name, factor in factors.items():
        out[name] = (out[name] * factor).astype(out[name].dtype)
    return out
```

```python
from contextlib import ExitStack, contextmanager

import concourse.bass as bass
from concourse import mybir

F32 = mybir.dt.float32
F32R = mybir.dt.float32r
ALU = mybir.AluOpType
ACT = mybir.ActivationFunctionType
AX_X = mybir.AxisListType.X

P = 128
D = 2048
KD = D // P
NT = 256
NB = 8
COLS = NT + NB
FF = 5632
KF = FF // P
NCHUNK = 2
KC = KF // NCHUNK
UPS = KC // 2
DNS = KD // 2
W = 1024
KW = W // P
NHEAD = 16
NSTATE = 128
CW = 4
CONV_C = W + 2 * 2 * NSTATE
KX = CONV_C // P
IN_COLS = 2 * W + W + CONV_C + NHEAD
EPS = 1e-6
PAIR = 256
PIECE = 4 * PAIR
CPAD = CW - 1 + NT + NB * CW
COUT = CPAD - (CW - 1)
SAMP0 = CW - 1 + NT

SH1, SC1, G1, SH2, SC2, G2, SH3, SC3, G3, SHF, SCF = range(11)
ADA_ORDER = [SH1, SC1, G1, SH2, SC2, G2, SH3, SC3, G3, SHF, SCF]

S_FF1 = 0
S_DT = S_FF1 + NCHUNK * (UPS + DNS)
S_XBC = S_DT + 1
S_LRU = S_XBC + KX // 4
S_Z = S_LRU + KW // 2
S_OUT = S_Z + KW // 4
S_FF2 = S_OUT + KD // 4
S_END = S_FF2 + NCHUNK * (UPS + DNS)

PIECES = {
    "full": [4] * 8,
    "down": [3, 3, 3, 3, 3, 3, 2, 2],
    "dt": [2] * 8,
}
WIDE = {"full": PAIR, "down": PAIR, "dt": P}
assert sum(PIECES["down"]) == KC and PIECE >= 4 * PAIR


def blocks_of_rows():
    return [
        ("c_prompt", KD), ("c_sample", NB * KD), ("b_ada", 9 * KD), ("b_ada_f", 2 * KD),
        ("x_sample", NB * KD), ("g_ffn1", KD), ("g_mix", KD), ("g_ffn2", KD), ("g_final", KD),
        ("lru_conv_w", CW * KW), ("lru_conv_b", KW), ("lru_ba", KW), ("lru_bi", KW),
        ("lru_lambda", KW), ("ssd_conv_w", CW * KX), ("ssd_conv_b", KX), ("ssd_norm_g", KW),
        ("state_lru_h", NB * KW), ("state_lru_conv", NB * (CW - 1) * KW),
        ("state_ssd_conv", NB * (CW - 1) * KX),
    ]


def packed(blocks):
    at, copies, row = {}, [], 0
    for name, n in blocks:
        at[name] = row
        done = 0
        while done < n:
            r = (row + done) % P
            m = min(n - done, P - r)
            copies.append((name, done, (row + done) // P, r, m))
            done += m
        row += n
    return at, copies, -(-row // P), row


ROW_AT, ROW_COPIES, ROW_TILES, ROWS = packed(blocks_of_rows())
C_TILES = -(-(9 * KD) // P)
OUT_BLOCKS = [
    ("lru_conv_prompt", (CW - 1) * KW), ("lru_conv_sample", NB * (CW - 1) * KW),
    ("ssd_conv_prompt", (CW - 1) * KX), ("ssd_conv_sample", NB * (CW - 1) * KX),
    ("lru_h_prompt", KW), ("lru_h_sample", NB * KW),
]
N_ROWB = -(-(ROW_TILES - C_TILES) // 4)
OTHER_ROWS = 16 * (len([c for c in ROW_COPIES if c[2] >= C_TILES]) + 3)
OUT_AT, OUT_COPIES, OUT_TILES, OUT_ROWS = packed(OUT_BLOCKS)


class Chain:

    def __init__(self, eng, sem):
        self.eng, self.sem, self.n = eng, sem, 0

    def add(self, ins):
        ins.then_inc(self.sem, 1)
        self.n = self.n + 1
        return self.n

    def wait(self, n=None):
        self.eng.wait_ge(self.sem, self.n if n is None else n)

    def link(self, ins):
        self.add(ins)
        self.wait()

    @contextmanager
    def loop(self, lo, hi, links):
        base = self.n
        with self.eng.Fori(lo, hi) as i:
            self.n = i * links + (base - lo * links)
            yield i
        self.n = base + (hi - lo) * links


def build(nc, ins, outs):
    with ExitStack() as ctx:
        def sb(name, shape, dt=F32):
            return ctx.enter_context(nc.sbuf_tensor(name, shape, dt))

        def sem(name):
            return ctx.enter_context(nc.semaphore(name))

        x = sb("x", [P, KD, COLS])
        h_hi = sb("h_hi", [P, KD, COLS], F32R)
        h_lo = sb("h_lo", [P, KD, COLS], F32R)
        raw = sb("raw", [P, 4, 2 * PIECE])
        w_hi = sb("w_hi", [P, 4, PIECE], F32R)
        w_lo = sb("w_lo", [P, 4, PIECE], F32R)
        small = sb("small", [P, ROW_TILES * P])
        mods = sb("mods", [P, 11, KD, 9])
        gain = sb("gain", [P, KD, 9])
        gate = sb("gate", [P, KD, 9])
        ident = sb("ident", [P, P])
        tri = sb("tri", [P, P])
        ones = sb("ones", [P, P])
        cT = sb("cT", [P, KD, 32])
        eps = sb("eps", [P, 1])
        rstd = sb("rstd", [P, COLS])
        sumsq = sb("sumsq", [P, 2, COLS])
        part = sb("part", [P, 2, COLS])
        part2 = sb("part2", [P, 2, COLS])
        samp = sb("samp", [P, KD, NB])
        silu_g = sb("silu_g", [P, 2, COLS])
        ntile = sb("ntile", [P, 4, NT])
        heads_row = sb("heads_row", [1, 3 * NHEAD])
        heads = sb("heads", [P, 3, NHEAD])
        outcol = sb("outcol", [P, OUT_TILES * P])

        base = nc.sbuf_base
        base = -(-base // 64) * 64
        room = nc.sbuf_usable_end - base

        def layout(entries):
            at, made = base, []
            for name, shape, dt in entries:
                made.append(nc.alloc_sbuf_tensor_at(name, shape, dt, offset=at))
                size = 4
                for n in shape[1:]:
                    size *= n
                at += -(-size // 32) * 32
            assert at <= base + room, (entries[0][0], at - base, room)
            return made

        ada, ada_sum, act_hi, act_lo = layout([
            ("ada", [P, 2, D], F32), ("ada_sum", [P, 512], F32),
            ("act_hi", [P, KC, COLS], F32R), ("act_lo", [P, KC, COLS], F32R)])
        _, _, rowbuf, xrows = layout([
            ("ada_s", [P, 2, D], F32), ("ada_sum_s", [P, 512], F32),
            ("rowbuf", [P, ROW_TILES, P], F32), ("xrows", [P, 2, D], F32)])
        _, _, yrows, ysrow = layout([
            ("ada_e", [P, 2, D], F32), ("ada_sum_e", [P, 512], F32),
            ("yrows", [P, 2, D], F32), ("ysrow", [P, P], F32)])
        (xbc, out_l, cin, cfull, cval, xdt, xdec, btok, cbm, s0, s0t, state, spread_b, spread_c,
         gates_w, th, rec, dA, spt, sp2, sp3, sp4, lam2, half_b, exp_a, cst, decl, tot, cdf, dfeat,
         dts_f, dcs_f, xsdt, zs) = layout([
            ("xbc", [P, KX, COLS], F32),
            ("out_l", [P, KW, COLS], F32),
            ("cin", [P, 2, 2, CPAD], F32), ("cfull", [P, 2, COUT], F32),
            ("cval", [P, 2, COLS], F32),
            ("xdt", [P, W], F32), ("xdec", [P, W], F32), ("btok", [P, 2, P], F32),
            ("cbm", [P, 2, P], F32), ("s0", [P, KW, P], F32), ("s0t", [P, W], F32),
            ("state", [P, 4, 4, NSTATE], F32), ("spread_b", [P, 4, NSTATE], F32),
            ("spread_c", [P, 4, NSTATE], F32), ("gates_w", [P, 2, KW, P], F32),
            ("th", [P, 2, 2, COLS], F32), ("rec", [P, 2, COLS], F32),
            ("dA", [P, 3, NHEAD], F32), ("spt", [P, 56], F32),
            ("sp2", [P, 56], F32), ("sp3", [P, 56], F32), ("sp4", [P, 56], F32),
            ("lam2", [P, KW], F32), ("half_b", [P, 2, KW], F32), ("exp_a", [P, NHEAD], F32),
            ("cst", [P, 2, NHEAD], F32), ("decl", [P, 2, NHEAD], F32), ("tot", [P, NHEAD], F32),
            ("cdf", [P, KW], F32), ("dfeat", [P, KW], F32),
            ("dts_f", [P, KW, NB], F32), ("dcs_f", [P, KW, NB], F32), ("xsdt", [P, KW, NB], F32),
            ("zs", [P, KW, NB], F32)])
        diag, prod = (ntile[:, 2 * a:2 * a + 2, :].rearrange("p a n -> p (a n)")
                      .rearrange("p (b n) -> p b n", n=NSTATE) for a in (0, 1))
        gel, aa = silu_g, part
        dtq = part2[:, 0, :]
        dexp = sumsq[0:NB, :, 0:P].rearrange("p a (b h) -> p a b h", h=NHEAD)
        outrow = xdt[:, 0:OUT_TILES * P].rearrange("p (a n) -> p a n", n=P)
        dmat = xdec[:, 0:4 * P].rearrange("p (r j n) -> p r j n", r=2, j=2)
        cexp = xdec[:, 4 * P:6 * P].rearrange("p (j n) -> p j n", j=2)

        main = ctx.enter_context(nc.psum_tensor("main", [P, 4, 512], F32))
        b4, b5, b6, b7 = (ctx.enter_context(nc.psum_tensor(f"b{n}", [P, 512], F32))
                          for n in range(4, 8))

        w_landed = [sem(f"w_landed{j}") for j in range(4)]
        ada_landed = [sem(f"ada_landed{j}") for j in range(2)]
        hi_done, lo_done = sem("hi_done"), sem("lo_done")
        piece_used = sem("piece_used")
        drained = [sem("drained_even"), sem("drained_odd")]
        ada_used, ada_copied = sem("ada_used"), sem("ada_copied")
        ada_turned, mod_ready = sem("ada_turned"), sem("mod_ready")
        act_ready = sem("act_ready")
        consts_ready = sem("consts_ready")
        c_rows, x_rows, other_rows = sem("c_rows"), sem("x_rows"), sem("other_rows")
        rows_turned, rows_placed, c_ready = sem("rows_turned"), sem("rows_placed"), sem("c_ready")
        heads_spread, heads_ready = sem("heads_spread"), sem("heads_ready")
        sumsq_ready, sumsq_spread, std_ready = sem("sumsq_ready"), sem("sumsq_spread"), sem("std_ready")
        aff_ready, hhi_ready, h_ready = sem("aff_ready"), sem("hhi_ready"), sem("h_ready")
        act_chain, dve_chain, pool_chain = sem("act_chain"), sem("dve_chain"), sem("pool_chain")
        dt_turned, cs_spread, dt_exp, dA_ready = sem("dt_turned"), sem("cs_spread"), sem("dt_exp"), sem("dA_ready")
        abs_ready, decl_sub, decl_ready, dexp_ready = sem("abs_ready"), sem("decl_sub"), sem("decl_ready"), sem("dexp_ready")
        samp_spread, samp_placed = sem("samp_spread"), sem("samp_placed")
        mix_init, gates_zero, gates_in = sem("mix_init"), sem("gates_zero"), sem("gates_in")
        hist_ready, captured = sem("hist_ready"), sem("captured")
        conv0_ready, conv_ready, xbc_ready = sem("conv0_ready"), sem("conv_ready"), sem("xbc_ready")
        prep_turned, prep_done = sem("prep_turned"), sem("prep_done")
        st_made, st_placed = sem("st_made"), sem("st_placed")
        bc_made, d_ready, e_ready, cexp_raw, m_ready = (sem(n) for n in (
            "bc_made", "d_ready", "e_ready", "cexp_raw", "m_ready"))
        y_made, y_placed = sem("y_made"), sem("y_placed")
        gate_made, gate_taken, decay_tanh, rec_ready, sqrt_ready, drive_ready, hl_ready, out_l_ready, ix_ready = (
            sem(n) for n in ("gate_made", "gate_taken", "decay_tanh", "rec_ready", "sqrt_ready",
                             "drive_ready", "hl_ready", "out_l_ready", "ix_ready"))
        gl_square, gl_inner, gl_tanh = sem("gl_square"), sem("gl_inner"), sem("gl_tanh")
        diag_ready, diag_spread, spread_done = sem("diag_ready"), sem("diag_spread"), sem("spread_done")
        st_in = [sem(f"st_in{i}") for i in range(4)]
        st_out = [sem(f"st_out{i}") for i in range(4)]
        st_new, st_prod, st_sum = sem("st_new"), sem("st_prod"), sem("st_sum")
        sz_ready = sem("sz_ready")
        out_turned, out_rows_ready, stored = sem("out_turned"), sem("out_rows_ready"), sem("stored")
        y_turned = sem("y_turned")
        y_rows_even, y_rows_odd = sem("y_rows_even"), sem("y_rows_odd")
        h_captured, xdt_ready = sem("h_captured"), sem("xdt_ready")

        w_up = [ins[n][0].rearrange("(k p) n -> p k n", p=P) for n in ("w_up1", "w_up2")]
        w_down = [ins[n][0].rearrange("(k p) n -> p k n", p=P) for n in ("w_down1", "w_down2")]
        w_in = ins["w_in"][0].rearrange("(k p) n -> p k n", p=P)
        w_out = ins["w_out"][0].rearrange("(k p) n -> p k n", p=P)
        w_ada = ins["w_ada"][0].rearrange("(k p) n -> p k n", p=P)
        w_ada_f = ins["w_ada_f"].rearrange("(k p) n -> p k n", p=P)
        ssm_in = ins["state_ssm"][0].rearrange("b (t q) p n -> t (q p) b n", q=2)
        ssm_out = outs["ssm_sample"][0].rearrange("b (t q) p n -> t (q p) b n", q=2)

        def rows_of(name):
            a = ins[name]
            flat = {1: "a -> (a)", 2: "a b -> (a b)", 3: "a b c -> (a b c)",
                    4: "a b c d -> (a b c d)"}[len(a.shape)]
            return (a if len(a.shape) == 1 else a.rearrange(flat)).rearrange("(r p) -> r p", p=P)

        def smallcol(name, n, at=0):
            return small[:, ROW_AT[name] + at:ROW_AT[name] + at + n]

        g_of = {n: smallcol(n, KD) for n in ("g_ffn1", "g_mix", "g_ffn2", "g_final")}

        plan = []

        def ffn_plan(f, s, e, o, vec, up_vecs, down_vecs):
            for c in range(NCHUNK):
                n = up_vecs[c]
                plan.append(("up", s, n, 4, vec, e, o, (f, c, 0)))
                plan.append(("up", s + 4 * n, UPS - 4 * n, 1, None, e + 4 * n, o + 4 * n, (f, c, 4 * n)))
                vec += n
                s, e, o = s + UPS, e + UPS, o + UPS
                done = 4 * down_vecs[c]
                if done:
                    plan.append(("down", s, 1, 4, vec, e, o, (f, c, 0)))
                plan.append(("down", s + done, (DNS - done) // 2, 2, None,
                             e + done // 2, o + done // 2, (f, c, done)))
                vec += down_vecs[c]
                s, e, o = s + DNS, e + DNS // 2, o + DNS // 2
            return s, e, o, vec

        s, e, o, vec = ffn_plan(0, 0, 0, 0, 2, (2, 2), (1, 1))
        assert s == S_DT
        plan.append(("dt", s, 1, 1, None, e, o, None))
        e += 1
        for what, n, first in (("xbc", S_LRU - S_XBC, S_XBC), ("lru", S_Z - S_LRU, S_LRU),
                               ("z", S_OUT - S_Z, S_Z), ("out", S_FF2 - S_OUT, S_OUT)):
            for t in range(n):
                plan.append((what, first + t, 1, 1, None, e, o, t))
                e, o = e + 1, o + 1
        s, e, o, vec = ffn_plan(1, S_FF2, e, o, vec, (1, 2), (0, 0))
        assert s == S_END and vec == 11
        E_MIX_FIRST = [g[5] for g in plan if g[0] == "xbc"][0]
        DRAIN_GL = [g[6] for g in plan if g[0] == "lru"][0]
        AFF_FINAL = 2 * (KD + 1) + KW + (KD + 1) + 1
        PIECE_KIND = {"up": "full", "down": "down", "dt": "dt", "xbc": "full", "lru": "full",
                      "z": "full", "out": "full"}

        def turns(eng, seg, peel_first=False, peel_last=False, chain=None, links=0):
            n = seg[2]
            lo, hi = int(peel_first), n - int(peel_last)
            for i in range(min(lo, n)):
                yield i, i == n - 1
            if hi - lo == 1:
                yield lo, lo == n - 1
            elif hi > lo:
                if chain is None:
                    with eng.Fori(lo, hi) as i:
                        yield i, False
                else:
                    with chain.loop(lo, hi, links) as i:
                        yield i, False
            for i in range(max(hi, lo), n):
                yield i, True

        def at_step(seg, i, k):
            kind, s0_, _, per, _, e0, o0, _ = seg
            s = i * per + (s0_ + k)
            if kind == "down":
                return s, i * (per // 2) + (e0 + (k + 1) // 2), i * (per // 2) + (o0 + k // 2), k % 2
            return s, i * per + (e0 + k), i * per + (o0 + k), 0

        def last_kind(n):
            return PIECE_KIND[plan[n + 1][0]] if n + 1 < len(plan) else None

        def differs(n):
            return last_kind(n) != PIECE_KIND[plan[n][0]]

        def unit_source(seg, i, k, j):
            kind, _, _, per, _, _, _, what = seg
            if kind == "up":
                f, c, at = what
                col = i * (per * PAIR) + ((c * UPS + at + k) * PAIR + (0 if j < 2 else FF))
                return w_up[f][:, 8 * (j % 2):8 * (j % 2) + 8, bass.ds(col, PAIR)]
            if kind == "down":
                f, c, at = what
                k0 = c * KC + sum(PIECES["down"][:2 * j])
                nk = sum(PIECES["down"][2 * j:2 * j + 2])
                return w_down[f][:, k0:k0 + nk, bass.ds(i * (per * PAIR) + (at + k) * PAIR, PAIR)]
            if kind == "dt":
                return w_in[:, 4 * j:4 * j + 4, IN_COLS - P:IN_COLS]
            t, half = what, j // 2
            col = {"xbc": 3 * W + (2 * t + half) * PAIR, "z": 2 * W + (2 * t + half) * PAIR,
                   "lru": t * PAIR + (0 if half == 0 else W), "out": (2 * t + half) * PAIR}[kind]
            w = w_out if kind == "out" else w_in
            return w[:, 8 * (j % 2):8 * (j % 2) + 8, col:col + PAIR]

        def raw_piece(m, kind):
            n, wide = PIECES[kind][m], WIDE[kind]
            first = PIECES[kind][m - 1] if m % 2 else 0
            return raw[:, m // 2, first * wide:(first + n) * wide]

        def split_view(t, m, kind):
            return t[:, m % 4, 0:PIECES[kind][m] * WIDE[kind]]

        def windows(r):
            return cin[:, r, :, SAMP0:SAMP0 + NB * CW].rearrange("p j (b w) -> p j b w", w=CW)

        def pair_of_conv(idx):
            if idx < 6:
                return S_XBC + idx // 2, idx % 2, E_MIX_FIRST + idx // 2 - (idx % 2)
            return S_LRU + idx - 6, 0, E_MIX_FIRST + 3 + idx - 6

        def cin_filled(idx):
            _, par, before = pair_of_conv(idx)
            return drained[par], before + 1

        def conv_params(idx, j):
            if idx < 6:
                t = 2 * idx + j
                return (lambda w: smallcol("ssd_conv_w", 1, w * KX + t)), smallcol("ssd_conv_b", 1, t)
            t = 2 * (idx - 6) + j
            return (lambda w: smallcol("lru_conv_w", 1, w * KW + t)), smallcol("lru_conv_b", 1, t)

        def sample_traffic(sp, q, j):
            if q >= 1 and q - 1 < 4:
                g, half = (q - 1) // 2, (q - 1) % 2
                sp.wait_ge(st_new, 4 * (q - 1) + j + 1)
                sp.dma_start(ssm_out[4 * g + j][:, 4 * half:4 * half + 4, :],
                             state[:, j, :, :]).then_inc(st_out[j], 16)
            if q < 4:
                g, half = q // 2, q % 2
                if q == 0:
                    sp.wait_ge(mix_init, 1)
                else:
                    sp.wait_ge(st_out[j], 16 * q)
                    sp.wait_ge(st_prod, 4 * (q - 1) + j + 1)
                sp.dma_start(state[:, j, :, :],
                             ssm_in[4 * g + j][:, 4 * half:4 * half + 4, :]).then_inc(st_in[j], 16)

        block = ctx.enter_context(nc.Block())

        @block.sync
        def _(sp):
            def ada_load(a, vec, k):
                if not isinstance(a, int) or a >= 2:
                    sp.wait_ge(ada_used, a - 1)
                if isinstance(vec, int) and vec >= SHF:
                    src = w_ada_f[:, k, (vec - SHF) * D:(vec - SHF + 1) * D]
                elif isinstance(vec, int):
                    src = w_ada[:, k, vec * D:(vec + 1) * D]
                else:
                    src = w_ada[:, k, bass.ds(vec * D, D)]
                sp.dma_start(ada[:, k % 2, :], src).then_inc(ada_landed[k % 2], 16)

            for vec in (SH1, SC1):
                for k in range(KD):
                    ada_load(vec * KD + k, vec, k)
            for n, seg in enumerate(plan):
                kind, s_first, _, per, vec0, _, _, what = seg
                dynamic_f = vec0 is not None and vec0 >= SHF
                for i, _ in turns(sp, seg, peel_first=s_first == 0 or dynamic_f, peel_last=dynamic_f):
                    for k in range(per):
                        s = at_step(seg, i, k)[0]
                        for j in range(4):
                            if not isinstance(s, int) or s >= 1:
                                sp.wait_ge(lo_done, s * 8 + (2 * j - 6))
                            wide = WIDE[PIECE_KIND[kind]]
                            nk = sum(PIECES[PIECE_KIND[kind]][2 * j:2 * j + 2])
                            dst = raw[:, j, 0:nk * wide].rearrange("p (k n) -> p k n", n=wide)
                            sp.dma_start(dst, unit_source(seg, i, k, j)).then_inc(w_landed[j], 16)
                            if vec0 is not None:
                                vec = i + vec0
                                if j == 0 and k == 0 and what[0] == 1 and what[2] == 0:
                                    sp.wait_ge(h_ready, 3 * KD)
                                ada_load(vec * KD + 4 * k + j, vec, 4 * k + j)
                            if kind in ("lru", "z"):
                                sample_traffic(sp, what + (KW // 2 if kind == "z" else 0), j)
            for q in range(4):
                sp.wait_ge(y_rows_even, q + 1)
                sp.wait_ge(y_rows_odd, q + 1)
                sp.dma_start(outs["y_prompt"][0].rearrange("(c p) n -> p c n", p=P)[:, :, q * 512:(q + 1) * 512],
                             yrows[:, :, q * 512:(q + 1) * 512]).then_inc(stored, 16)
            sp.wait_ge(y_rows_even, 5)
            sp.dma_start(outs["y_sample"].rearrange("b s (t p) -> (b s t) p", p=P),
                         ysrow[:, :]).then_inc(stored, 16)
            for i in range(4):
                sp.wait_ge(st_out[i], 16 * 4)
            sp.wait_ge(stored, 16 * (len(OUT_COPIES) + 1 + 5))

        @block.gpsimd
        def _(pool):
            ch = Chain(pool, pool_chain)
            ch.link(pool.memset(ident[:, :], 0.0))
            ch.link(pool.affine_select(out=ident[:, :], in_=ident[:, :], compare_op=ALU.not_equal,
                                       fill=1.0, base=0, pattern=[[-1, P]], channel_multiplier=1))
            ch.link(pool.memset(ones[:, :], 1.0))
            pool.memset(eps[:, :], EPS)
            pool.memset(cT[:, :, :], 0.0)
            pool.memset(outcol[:, OUT_ROWS:], 0.0)
            pool.affine_select(out=tri[:, :], in_=ones[:, :], compare_op=ALU.is_ge, fill=0.0,
                               base=0, pattern=[[1, P]], channel_multiplier=-1).then_inc(consts_ready, 1)
            pool.wait_ge(piece_used, 8 * S_DT)
            pool.memset(spt[:, :], 0.0)
            pool.memset(cin[:, :, :, 0:CW - 1], 0.0).then_inc(mix_init, 1)
            pool.memset(gates_w[:, :, :, :], 0.0).then_inc(gates_zero, 1)

            def history(idx):
                name, t, kk = ("state_ssd_conv", 2 * idx, KX) if idx < 6 else \
                    ("state_lru_conv", 2 * (idx - 6), KW)
                if idx >= 2:
                    pool.wait_ge(captured, idx - 1)
                    pool.wait_ge(conv_ready, 2 * (idx - 1))
                src = smallcol(name, NB * 3 * kk).rearrange("p (b w t) -> p t b w", w=3, t=kk)
                for j in range(2):
                    ins_ = pool.tensor_copy(windows(idx % 2)[:, j, :, 0:3], src[:, t + j, :, :])
                ins_.then_inc(hist_ready, 1)

            def capture(idx):
                kk, t, a, b = (KX, 2 * idx, "ssd_conv_prompt", "ssd_conv_sample") if idx < 6 else \
                    (KW, 2 * (idx - 6), "lru_conv_prompt", "lru_conv_sample")
                pool.wait_ge(*cin_filled(idx))
                pool.wait_ge(hist_ready, idx + 1)
                for j in range(2):
                    dst = outcol[:, OUT_AT[a]:OUT_AT[a] + 3 * kk].rearrange("p (w t) -> p t w", t=kk)
                    pool.tensor_copy(dst[:, t + j, :], cin[:, idx % 2, j, NT:NT + 3])
                    dst = outcol[:, OUT_AT[b]:OUT_AT[b] + NB * 3 * kk].rearrange(
                        "p (b w t) -> p t b w", w=3, t=kk)
                    ins_ = pool.tensor_copy(dst[:, t + j, :, :], windows(idx % 2)[:, j, :, 1:4])
                ins_.then_inc(captured, 1)

            history(0)
            history(1)
            for idx in range(6):
                capture(idx)
                history(idx + 2)

            def sample_item(q, i):
                g, half = q // 2, q % 2
                t, n = 4 * g + i, 4 * q + i
                bs = slice(4 * half, 4 * half + 4)
                st = state[:, i, :, :]
                pool.wait_ge(st_in[i], 16 * (q + 1))
                ch.link(pool.tensor_tensor(st, st, dcs_f[:, t, bs].unsqueeze(2).to_broadcast([P, 4, NSTATE]), ALU.mult))
                pool.wait_ge(spread_done, 2 * q + 1)
                if n:
                    pool.wait_ge(st_sum, n)
                ch.link(pool.tensor_tensor(prod, spread_b[:, :, :],
                                           xsdt[:, t, bs].unsqueeze(2).to_broadcast([P, 4, NSTATE]), ALU.mult))
                pool.tensor_tensor(st, st, prod, ALU.add).then_inc(st_new, 1)
                pool.wait_ge(st_new, n + 1)
                pool.wait_ge(spread_done, 2 * q + 2)
                pool.tensor_tensor(prod, st, spread_c[:, :, :], ALU.mult).then_inc(st_prod, 1)

            pool.wait_ge(samp_placed, 2)
            for q in range(4):
                sample_item(q, 0)
                capture(6 + q)
                if q < 2:
                    history(8 + q)
                sample_item(q, 1)
                pool.wait_ge(gate_taken, 2 * (2 * q + 2))
                ch.link(pool.tensor_scalar(th[:, 1, :, :], th[:, 1, :, :], 0.5, 0.5, ALU.mult, ALU.add))
                pool.tensor_tensor(th[:, 1, :, :], th[:, 1, :, :], cval[:, :, :], ALU.mult).then_inc(ix_ready, 1)
                sample_item(q, 2)
                pool.wait_ge(ix_ready, q + 1)
                pool.wait_ge(sqrt_ready, q + 1)
                ch.link(pool.tensor_tensor(th[:, 0, :, :], th[:, 0, :, :], rec[:, :, :], ALU.mult))
                pool.tensor_tensor(th[:, 0, :, :], th[:, 0, :, :], th[:, 1, :, :], ALU.mult).then_inc(drive_ready, 1)
                sample_item(q, 3)
                pool.wait_ge(hl_ready, q + 1)
                pool.tensor_copy(outcol[:, OUT_AT["lru_h_prompt"] + 2 * q:OUT_AT["lru_h_prompt"] + 2 * q + 2],
                                 rec[:, :, NT - 1])
                dst = outcol[:, OUT_AT["lru_h_sample"]:OUT_AT["lru_h_sample"] + NB * KW].rearrange(
                    "p (b t) -> p t b", t=KW)
                pool.tensor_copy(dst[:, 2 * q:2 * q + 2, :], rec[:, :, NT:COLS]).then_inc(h_captured, 1)

        @block.scalar
        def _(act):
            ch = Chain(act, act_chain)
            A = nc.scalar.activation

            def hi_piece(s, m, kind):
                v = s * 8 + m
                act.wait_ge(w_landed[m // 2], s * 16 + 16)
                if not isinstance(v, int) or v >= 4:
                    act.wait_ge(piece_used, v - 3)
                A(split_view(w_hi, m, kind), raw_piece(m, kind), ACT.Copy).then_inc(hi_done, 1)

            def pieces_ahead(s, j, kind, nxt):
                for m in (2 * j + 3, 2 * j + 4):
                    if m < 8:
                        hi_piece(s, m, kind)
                    elif nxt is not None:
                        hi_piece(s + 1, m - 8, nxt)

            def ada_copy(vec):
                act.wait_ge(ada_used, vec * KD + KD)
                A(ada_sum[:, :], b4[:, :], ACT.Copy).then_inc(ada_copied, 1)

            def norm_std(n, width):
                act.wait_ge(sumsq_spread, n)
                A(rstd[:, :], b6[:, 0:COLS], ACT.Sqrt, bias=eps[:, 0:1], scale=1.0 / width).then_inc(std_ready, 1)

            def norm_hi(n, a0, h0, inserts=()):
                act.wait_ge(aff_ready, a0 + 1)
                A(h_hi[:, :, NT:COLS], samp[:, :, :], ACT.Copy).then_inc(hhi_ready, 1)
                for k in range(KD):
                    act.wait_ge(aff_ready, a0 + 2 + k)
                    A(h_hi[:, k, 0:NT], ntile[:, k % 4, :], ACT.Copy).then_inc(hhi_ready, 1)
                    if k in inserts:
                        hi_piece(0, inserts[k], "full")

            def row_copies(names, s):
                for name, r, tile, at, m in ROW_COPIES:
                    if (tile < C_TILES) == names:
                        act.dma_start(rowbuf[at:at + m, tile, :], rows_of(name)[r:r + m, :]).then_inc(s, 16)
            row_copies(True, c_rows)
            for c in range(2):
                act.dma_start(xrows[:, c, :], ins["x_prompt"][0, c * P:(c + 1) * P, :]).then_inc(x_rows, 16)
            row_copies(False, other_rows)
            for n, name in enumerate(("ssd_dt_bias", "ssd_A_log", "ssd_D")):
                act.dma_start(heads_row[0:1, n * NHEAD:(n + 1) * NHEAD], ins[name]).then_inc(other_rows, 16)
            act.wait_ge(rows_placed, 1)
            act.wait_ge(consts_ready, 1)
            A(cT[:, :, 0:9], small[:, 0:9 * KD].rearrange("p (r k) -> p k r", k=KD), ACT.Silu).then_inc(c_ready, 1)
            ada_copy(SH1)
            ada_copy(SC1)
            norm_std(1, D)
            norm_hi(0, 0, 0, {3: 0, 7: 1, 11: 2})

            def conv_first(idx):
                step, par, before = pair_of_conv(idx)
                r = idx % 2
                act.wait_ge(piece_used, 8 * step + (8 if par else 4))
                if idx < 2:
                    act.wait_ge(mix_init, 1)
                else:
                    act.wait_ge(captured, idx - 1)
                    act.wait_ge(conv_ready, 2 * (idx - 1))
                A(cin[:, r, :, CW - 1:SAMP0], main[:, 2 * par:2 * par + 2, 0:NT], ACT.Copy)
                A(windows(r)[:, :, :, CW - 1], main[:, 2 * par:2 * par + 2, NT:COLS], ACT.Copy).then_inc(drained[par], 1)
                act.wait_ge(drained[par], before + 1)
                act.wait_ge(hist_ready, idx + 1)
                if idx:
                    act.wait_ge(conv_ready, 2 * idx)
                for j in range(2):
                    w, b = conv_params(idx, j)
                    A(cfull[:, j, :], cin[:, r, j, 0:COUT], ACT.Identity, bias=b,
                      scale=w(0)).then_inc(conv0_ready, 1)

            def xbc_silu(idx):
                act.wait_ge(conv_ready, 2 * (idx + 1))
                A(xbc[:, 2 * idx:2 * idx + 2, :], cval[:, :, :], ACT.Silu).then_inc(xbc_ready, 1)

            def item_exp(k):
                act.wait_ge(d_ready, k + 1)
                if k >= 8:
                    A(cexp, b5[:, 0:2 * P].rearrange("p (j n) -> p j n", j=2), ACT.Exp).then_inc(cexp_raw, 1)
                A(dmat[:, k % 2, :, :], dmat[:, k % 2, :, :], ACT.Exp).then_inc(e_ready, 1)

            def gate_tanh(t):
                act.wait_ge(gate_made, t + 1)
                if t % 2 == 0 and t:
                    act.wait_ge(hl_ready, t // 2)
                for gt, bank in ((0, b4), (1, b7)):
                    A(th[:, gt, t % 2, :], bank[:, 0:COLS], ACT.Tanh, bias=half_b[:, gt, t:t + 1],
                      scale=0.5).then_inc(gate_taken, 1)

            def spread_copy(n, dst):
                act.wait_ge(diag_spread, n + 1)
                if n >= 2:
                    act.wait_ge(st_prod, 4 * (n // 2))
                A(dst.rearrange("p b n -> p (b n)"), b7[:, :], ACT.Copy).then_inc(spread_done, 1)

            def act_tasks(kind, t, j):
                u = 4 * t + j
                if kind == "dt" and j == 3:
                    act.wait_ge(piece_used, 8 * S_DT + 8)
                    A(dtq, main[:, 0, 0:COLS], ACT.Copy).then_inc(drained[0], 1)
                    act.wait_ge(gates_zero, 1)
                    for gt, name in enumerate(("lru_wa", "lru_wi")):
                        for half in range(2):
                            o64 = 64 * half
                            act.dma_start(gates_w[o64:o64 + 64, gt, :, o64:o64 + 64],
                                          ins[name][0].rearrange("(t q) i j -> q i t j", q=2)[half]).then_inc(gates_in, 16)
                if kind == "xbc":
                    if j in (0, 2) and (t or j):
                        xbc_silu(2 * t + j // 2 - 1)
                    if j in (1, 3):
                        conv_first(2 * t + j // 2)
                    if u == 1:
                        act.wait_ge(abs_ready, 1)
                        A(sp3[:, :], sp2[:, :], ACT.Exp, scale=-1.0)
                        A(exp_a[:, :], heads[:, 1, :], ACT.Exp).then_inc(dt_exp, 1)
                    if u == 5:
                        act.wait_ge(decl_sub, 1)
                        A(decl[:, :, :], decl[:, :, :], ACT.Exp)
                        A(tot[:, :], b7[:, 48:64], ACT.Exp)
                        A(sp4[0:NB, 0:NHEAD], dA[0:NB, 2, :], ACT.Exp).then_inc(decl_ready, 1)
                if kind in ("lru", "z"):
                    r = u + (16 if kind == "z" else 0)
                    if r == 0:
                        xbc_silu(5)
                    if r == 2:
                        for g in range(2):
                            act.wait_ge(st_made, 1)
                            A(s0t[:, g * 512:(g + 1) * 512], (b5, b6)[g][:, :], ACT.Copy).then_inc(st_placed, 1)
                    if r == 3:
                        act.wait_ge(st_made, 2)
                        for g in range(2):
                            A(s0[:, 4 * g:4 * g + 4, :], (b5, b6)[g][:, :].rearrange("p (t n) -> p t n", n=P),
                              ACT.Copy).then_inc(st_placed, 1)
                    if 4 <= r <= 11:
                        item_exp(r - 4)
                    if 15 <= r <= 22:
                        item_exp(r - 7)
                if kind == "lru":
                    if j == 1:
                        conv_first(6 + t)
                    if j >= 2:
                        gate_tanh(2 * t + j - 2)
                    if j == 3:
                        act.wait_ge(gate_taken, 4 * (t + 1))
                        for h in range(2):
                            A(th[:, 0, h, :], th[:, 0, h, :], ACT.Tanh, bias=lam2[:, 2 * t + h:2 * t + h + 1],
                              scale=lam2[:, 2 * t + h:2 * t + h + 1]).then_inc(decay_tanh, 1)
                        act.wait_ge(piece_used, 8 * (S_LRU + t) + 8)
                        if t:
                            act.wait_ge(out_l_ready, t)
                        A(gel[:, :, :], main[:, 2:4, 0:COLS], ACT.Square).then_inc(gl_square, 1)
                if (kind == "lru" and j == 0 and t) or (kind == "z" and u == 0):
                    q = t - 1 if kind == "lru" else 3
                    act.wait_ge(gl_inner, q + 1)
                    A(gel[:, :, :], gel[:, :, :], ACT.Tanh, scale=0.7978845608028654).then_inc(gl_tanh, 1)
                    act.wait_ge(rec_ready, q + 1)
                    A(th[:, 0, :, :], th[:, 0, :, :], ACT.Sqrt, scale=4.0).then_inc(sqrt_ready, 1)
                if kind == "lru" and j < 2:
                    spread_copy(2 * t + j, (spread_b, spread_c)[j][:, :, :])
                if kind == "z" and j in (1, 3):
                    p_, par = 2 * t + j // 2, j // 2
                    act.wait_ge(piece_used, 8 * (S_Z + t) + (8 if par else 4))
                    act.wait_ge(out_l_ready, 4)
                    if p_:
                        act.wait_ge(sz_ready, p_)
                    A(silu_g[:, :, :], main[:, 2 * par:2 * par + 2, 0:COLS], ACT.Silu).then_inc(drained[par], 1)
                if kind == "z" and u == 7:
                    act.wait_ge(piece_used, 8 * S_OUT)
                    for k in range(KW):
                        A(h_hi[:, k, :], out_l[:, k, :], ACT.Copy).then_inc(hhi_ready, 1)
                    norm_std(3, W)
                    for k in range(KW):
                        act.wait_ge(aff_ready, 2 * 17 + k + 1)
                        A(h_hi[:, KW + k, :], xbc[:, k, :], ACT.Copy).then_inc(hhi_ready, 1)
                if kind == "out":
                    if u == 1:
                        act.wait_ge(out_turned, 2)
                        A(outrow[:, 0:4, :], b5[:, :].rearrange("p (a n) -> p a n", n=P), ACT.Copy)
                        A(outrow[:, 4, :], b6[:, 0:P], ACT.Copy).then_inc(out_rows_ready, 1)
                        act.wait_ge(out_rows_ready, 1)
                        for name, r, tile, at, m in OUT_COPIES:
                            dst = outs[name].rearrange({3: "a b c -> (a b c)", 4: "a b c d -> (a b c d)"}[
                                len(outs[name].shape)]).rearrange("(r p) -> r p", p=P)
                            act.dma_start(dst[r:r + m, :], outrow[at:at + m, tile, :]).then_inc(stored, 16)
                        act.wait_ge(prep_done, 3)
                        act.dma_start(outs["ssm_prompt"][0, 0].rearrange("(t q) p n -> (q p) t n", q=2),
                                      s0[:, :, :]).then_inc(stored, 16)
                if kind == "out" and u == 15:
                    norm_std(4, D)
                    norm_hi(3, 2 * 17 + KW, 2 * 17 + KD)

            up_done = 0
            for n, seg in enumerate(plan):
                kind, s_first, count, per, vec0, _, _, what = seg
                nxt = last_kind(n)
                for i, last in turns(act, seg, peel_first=n == 0, peel_last=differs(n)):
                    for k in range(per):
                        s, e_, o_, par = at_step(seg, i, k)
                        follows = nxt if last and k == per - 1 else PIECE_KIND[kind]
                        for j in range(4):
                            pieces_ahead(s, j, PIECE_KIND[kind], follows)
                            if kind == "up" and j == 1:
                                act.wait_ge(piece_used, s * 8 + 4)
                                act.wait_ge(drained[1], o_)
                                A(silu_g[:, :, :], main[:, 0:2, 0:COLS], ACT.Silu).then_inc(drained[0], 1)
                            if kind not in ("up", "down"):
                                act_tasks(kind, what or 0, j)
                    if vec0 is not None:
                        ada_copy(i + vec0)
                if kind == "down" and what[0] == 0 and what[1] == 1 and plan[n + 1][0] == "dt":
                    norm_std(2, D)
                    norm_hi(1, 17, 17)
            norm_std(5, D)
            for q in range(0, KW, 2):
                act.wait_ge(y_turned, q + 1)
                A(yrows[:, :, q * PAIR:(q + 1) * PAIR],
                  main[:, q % 4, :].rearrange("p (c n) -> p c n", c=2), ACT.Copy).then_inc(y_rows_even, 1)
            act.wait_ge(y_turned, KW + 1)
            A(ysrow[:, :], b7[:, 0:P], ACT.Copy).then_inc(y_rows_even, 1)

        @block.vector
        def _(dve):
            ch = Chain(dve, dve_chain)
            TT, TS, STT = dve.tensor_tensor, dve.tensor_scalar, dve.scalar_tensor_tensor

            def lo_piece(s, m, kind):
                v = s * 8 + m
                dve.wait_ge(hi_done, v + 1)
                TT(split_view(w_lo, m, kind), raw_piece(m, kind),
                   split_view(w_hi, m, kind).bitcast(F32), ALU.subtract).then_inc(lo_done, 1)

            def pieces_ahead(s, j, kind, nxt):
                for m in (2 * j + 3, 2 * j + 4):
                    if m < 8:
                        lo_piece(s, m, kind)
                    elif nxt is not None:
                        lo_piece(s + 1, m - 8, nxt)

            def mod_place(vec):
                dve.wait_ge(ada_turned, vec + 1)
                src = b4[:, :].rearrange("p (q j r) -> p q j r", q=4, j=4)[:, :, :, 0:9]
                dst = mods[:, bass.ds(vec, 1), :, :].rearrange("p a (j q) r -> p (a q) j r", q=4)
                bias = small[:, bass.ds(vec * KD + ROW_AT["b_ada"], KD)].rearrange(
                    "p (j q) -> p q j", q=4).unsqueeze(3).to_broadcast([P, 4, 4, 9])
                for q in range(4):
                    ins_ = TT(dst[:, q, :, :], src[:, q, :, :], bias[:, q, :, :], ALU.add)
                ins_.then_inc(mod_ready, 1)

            def make_gain(vec, name):
                dve.wait_ge(mod_ready, vec + 1)
                ch.link(STT(gain[:, :, :], mods[:, vec, :, :], 1.0,
                            g_of[name].unsqueeze(2).to_broadcast([P, KD, 9]), ALU.add, ALU.mult))

            def make_gate(vec, factor):
                dve.wait_ge(mod_ready, vec + 1)
                ch.link(TS(gate[:, :, :], mods[:, vec, :, :], factor, None, ALU.mult))

            def norm_samples(n, shift):
                dve.wait_ge(std_ready, n)
                ch.link(dve.reciprocal(rstd[:, :], rstd[:, :]))
                ch.link(TT(samp[:, :, :], x[:, :, NT:COLS],
                           rstd[:, NT:COLS].unsqueeze(1).to_broadcast([P, KD, NB]), ALU.mult))
                ch.link(TT(samp[:, :, :], samp[:, :, :], gain[:, :, 1:9], ALU.mult))

            def norm(n, shift, a0, h0, inserts=()):
                norm_samples(n, shift)
                TT(samp[:, :, :], samp[:, :, :], mods[:, shift, :, 1:9], ALU.add).then_inc(aff_ready, 1)

                def lo(k):
                    dve.wait_ge(hhi_ready, a0 + 2 + k)
                    TT(h_lo[:, k, 0:NT], ntile[:, k % 4, :], h_hi[:, k, 0:NT].bitcast(F32),
                       ALU.subtract).then_inc(h_ready, 1)
                for k in range(KD):
                    if k >= 4:
                        dve.wait_ge(h_ready, h0 + k - 3)
                    mark = ch.add(TT(ntile[:, k % 4, :], x[:, k, 0:NT], rstd[:, 0:NT], ALU.mult))
                    if k == 1:
                        dve.wait_ge(hhi_ready, a0 + 1)
                        TT(h_lo[:, :, NT:COLS], samp[:, :, :], h_hi[:, :, NT:COLS].bitcast(F32), ALU.subtract)
                    if k >= 1:
                        lo(k - 1)
                    ch.wait(mark)
                    TS(ntile[:, k % 4, :], ntile[:, k % 4, :], gain[:, k, 0:1], mods[:, shift, k, 0:1],
                       ALU.mult, ALU.add).then_inc(aff_ready, 1)
                    if k in inserts:
                        lo_piece(0, inserts[k], "full")
                lo(KD - 1)

            def add_branch(s, par, before, n0, squares):
                dve.wait_ge(piece_used, s)
                ps = main[:, 2 * par:2 * par + 2, :]
                ch.add(TT(part[:, :, 0:NT], ps[:, :, 0:NT],
                          gate[:, bass.ds(n0, 2), 0:1].to_broadcast([P, 2, NT]), ALU.mult))
                TT(part[:, :, NT:COLS], ps[:, :, NT:COLS], gate[:, bass.ds(n0, 2), 1:9],
                   ALU.mult).then_inc(drained[par], 1)
                dve.wait_ge(drained[par], before + 1)
                xs = x[:, bass.ds(n0, 2), :]
                ch.link(TT(xs, xs, part[:, :, :], ALU.add))
                if squares:
                    ch.link(TT(part2[:, :, :], xs, xs, ALU.mult))
                    ch.link(TT(sumsq[:, :, :], sumsq[:, :, :], part2[:, :, :], ALU.add))

            def place(b):
                bank = (b5, b6)[b % 2]
                dve.wait_ge(rows_turned, b + 1)
                if b == 0:
                    dve.tensor_copy(small[:, 0:C_TILES * P], bank[:, 0:C_TILES * P]).then_inc(rows_placed, 1)
                elif b <= N_ROWB:
                    lo_r, hi_r = (C_TILES + 4 * (b - 1)) * P, min((C_TILES + 4 * b) * P, ROWS)
                    dve.tensor_copy(small[:, lo_r:hi_r], bank[:, 0:hi_r - lo_r]).then_inc(rows_placed, 1)
                else:
                    k = 2 * (b - 1 - N_ROWB)
                    dve.tensor_copy(x[:, k:k + 2, 0:NT], bank[:, :].rearrange("p (k n) -> p k n", k=2)).then_inc(rows_placed, 1)
            for b in range(1 + N_ROWB + KD // 2):
                place(b)
            dve.wait_ge(rows_placed, 1 + N_ROWB + KD // 2)
            ch.link(dve.tensor_copy(x[:, :, NT:COLS], smallcol("x_sample", NB * KD).rearrange("p (b k) -> p k b", k=KD)))
            dve.wait_ge(heads_spread, 1)
            ch.link(dve.tensor_copy(heads[:, :, :], b7[:, 0:3 * NHEAD].rearrange("p (a h) -> p a h", a=3)))
            ch.link(dve.memset(sumsq[:, :, :], 0.0))
            for k in range(0, KD, 2):
                ch.link(TT(part2[:, :, :], x[:, k:k + 2, :], x[:, k:k + 2, :], ALU.mult))
                if k < KD - 2:
                    ch.link(TT(sumsq[:, :, :], sumsq[:, :, :], part2[:, :, :], ALU.add))
                else:
                    TT(sumsq[:, :, :], sumsq[:, :, :], part2[:, :, :], ALU.add).then_inc(sumsq_ready, 1)
            mod_place(SH1)
            mod_place(SC1)
            make_gain(SC1, "g_ffn1")
            norm(1, SH1, 0, 0, {3: 0, 7: 1, 11: 2})

            def conv_taps(idx):
                r = idx % 2
                if 0 < idx <= 6:
                    dve.wait_ge(xbc_ready, idx)
                elif idx > 6:
                    dve.wait_ge(ix_ready, idx - 6)
                    dve.wait_ge(gate_made, 2 * (idx - 6))
                for w in (1, 2):
                    for j in range(2):
                        dve.wait_ge(conv0_ready, 2 * idx + j + 1)
                        if w == 2:
                            ch.wait(marks[j])
                        tap, _ = conv_params(idx, j)
                        mark = ch.add(STT(cfull[:, j, :], cin[:, r, j, w:w + COUT], tap(w),
                                          cfull[:, j, :], ALU.mult, ALU.add))
                        marks = [mark] if j == 0 and w == 1 else marks + [mark]
                ch.wait()
                for j in range(2):
                    tap, _ = conv_params(idx, j)
                    STT(cval[:, j, 0:NT], cin[:, r, j, 3:3 + NT], tap(3), cfull[:, j, 0:NT], ALU.mult, ALU.add)
                    win = cfull[:, j, SAMP0 - 0:SAMP0 + 4 * NB - 3:4]
                    STT(cval[:, j, NT:COLS], windows(r)[:, j, :, 3], tap(3), win,
                        ALU.mult, ALU.add).then_inc(conv_ready, 1)

            def halves(dst, src_of):
                for q in range(2):
                    last = dve.tensor_copy(dst[64 * q:64 * q + 64], src_of(q))
                return last

            def prep(c):
                dve.wait_ge(prep_turned, c + 1)
                dve.tensor_copy(btok[:, :, :], b4[:, 0:2 * P].rearrange("p (g n) -> p g n", g=2))
                TT(cbm[:, :, :], b4[:, 2 * P:4 * P].rearrange("p (g n) -> p g n", g=2),
                   tri[:, :].unsqueeze(1).to_broadcast([P, 2, P]), ALU.mult)
                for g in range(2):
                    TT(xdt[:, g * 512:(g + 1) * 512].rearrange("p (h n) -> p h n", n=64),
                       (b5, b6)[g][:, :].rearrange("p (h n) -> p h n", n=64),
                       spt[:, c * NHEAD + 8 * g:c * NHEAD + 8 * g + 8].unsqueeze(2).to_broadcast([P, 8, 64]),
                       ALU.mult).then_inc(xdt_ready, 1)
                dve.wait_ge(xdt_ready, 2 * c + 2)
                TT(xdec[:, :].rearrange("p (h n) -> p h n", n=64), xdt[:, :].rearrange("p (h n) -> p h n", n=64),
                   decl[:, c, :].unsqueeze(2).to_broadcast([P, NHEAD, 64]), ALU.mult).then_inc(prep_done, 1)

            def item_decay(k):
                c, t = k // 8, k % 8
                dve.wait_ge(bc_made, k + 1)
                for j in range(2):
                    ins_ = TS(dmat[:, k % 2, j, :], b5[:, j * P:(j + 1) * P],
                              cst[:, c, 2 * t + j:2 * t + j + 1], 0.0, ALU.subtract, ALU.min)
                ins_.then_inc(d_ready, 1)

            def item_m(k):
                c, t = k // 8, k % 8
                g = t // 4
                if k >= 8:
                    dve.wait_ge(cexp_raw, k - 7)
                    TT(cexp, cexp, xbc[:, 10 + g, c * P:(c + 1) * P].unsqueeze(1).to_broadcast([P, 2, P]), ALU.mult)
                dve.wait_ge(e_ready, k + 1)
                TT(dmat[:, k % 2, :, :], dmat[:, k % 2, :, :],
                   cbm[:, g, :].unsqueeze(1).to_broadcast([P, 2, P]), ALU.mult).then_inc(m_ready, 1)

            def item_y(k):
                c, t = k // 8, k % 8
                dve.wait_ge(y_made, k + 1)
                v = xbc[:, t, c * P:(c + 1) * P]
                STT(v, v, dfeat[:, t:t + 1], b6[:, 0:P], ALU.mult, ALU.add).then_inc(y_placed, 1)

            def make_diag(n):
                q, cc = n // 2, n % 2
                g, half = q // 2, q % 2
                if n:
                    dve.wait_ge(diag_spread, n)
                src = xbc[:, 8 + 2 * cc + g, NT + 4 * half:NT + 4 * half + 4]
                TT(diag, ident[:, :].unsqueeze(1).to_broadcast([P, 4, P]),
                   src.unsqueeze(2).to_broadcast([P, 4, P]), ALU.mult).then_inc(diag_ready, 1)

            def sum_item(n):
                q, i = n // 4, n % 4
                g, half = q // 2, q % 2
                dve.wait_ge(st_prod, n + 1)
                dve.tensor_reduce(samp[:, 4 * g + i, 4 * half:4 * half + 4], prod, AX_X, ALU.add).then_inc(st_sum, 1)

            def dve_tasks(kind, t, j, s, o_, e_):
                u = 4 * t + j
                if kind == "xbc":
                    if j in (1, 3):
                        conv_taps(2 * t + j // 2)
                    if u == 0:
                        dve.wait_ge(dt_turned, 1)
                        dve.wait_ge(mix_init, 1)
                        TT(spt[:, 0:32].rearrange("p (c h) -> p c h", c=2),
                           b6[:, 0:2 * P].rearrange("p (c h) -> p c h", c=2)[:, :, P - NHEAD:P],
                           heads[:, 0:1, :].to_broadcast([P, 2, NHEAD]), ALU.add)
                        TT(spt[0:NB, 32:48], b6[0:NB, 3 * P - NHEAD:3 * P], heads[0:NB, 0, :], ALU.add)
                        ch.link(TS(spt[:, 48:56], smallcol("lru_lambda", KW), -1.0, None, ALU.mult))
                        STT(sp2[:, :], spt[:, :], -1.0, spt[:, :], ALU.mult, ALU.max).then_inc(abs_ready, 1)
                    if u == 1:
                        dve.wait_ge(dt_exp, 1)
                        ch.link(TS(sp2[:, :], sp3[:, :], 2.0, None, ALU.add))
                        ch.link(dve.reciprocal(sp2[:, :], sp2[:, :]))
                        ch.link(TT(sp2[:, :], sp2[:, :], sp3[:, :], ALU.mult))
                        ch.link(TT(sp3[:, :], sp2[:, :], sp2[:, :], ALU.mult))
                        ch.link(TS(sp4[:, :], sp3[:, :], 1.0 / 17, None, ALU.mult))
                        for odd in (15, 13, 11, 9, 7, 5, 3):
                            ch.link(STT(sp4[:, :], sp4[:, :], 1.0 / odd, sp3[:, :], ALU.add, ALU.mult))
                        ch.link(STT(sp4[:, :], sp4[:, :], 1.0, sp2[:, :], ALU.add, ALU.mult))
                        ch.link(TS(spt[:, :], spt[:, :], 0.0, None, ALU.max))
                        ch.link(STT(spt[:, :], sp4[:, :], 2.0, spt[:, :], ALU.mult, ALU.add))
                        TS(lam2[:, :], spt[:, 48:56], 2.0, None, ALU.mult)
                        TS(half_b[:, 0, :], smallcol("lru_ba", KW), 0.5, None, ALU.mult)
                        TS(half_b[:, 1, :], smallcol("lru_bi", KW), 0.5, None, ALU.mult)
                        STT(dA[:, :, :], spt[:, 0:48].rearrange("p (c h) -> p c h", c=3), -1.0,
                            exp_a[:, :].unsqueeze(1).to_broadcast([P, 3, NHEAD]), ALU.mult, ALU.mult).then_inc(dA_ready, 1)
                    if u == 4:
                        dve.wait_ge(cs_spread, 1)
                        ch.link(dve.tensor_copy(cst[:, :, :], b7[:, 0:32].rearrange("p (c h) -> p c h", c=2)))
                        TT(decl[:, :, :], b7[:, 32:64].rearrange("p (c h) -> p c h", c=2), cst[:, :, :],
                           ALU.subtract).then_inc(decl_sub, 1)
                    if u == 5:
                        dve.wait_ge(decl_ready, 1)
                        halves(cdf, lambda q: tot[64 * q:64 * q + 64, q:NHEAD:2])
                        halves(dfeat, lambda q: heads[64 * q:64 * q + 64, 2, q:NHEAD:2])
                        idb = ident[0:NB, 0:NB].unsqueeze(2).to_broadcast([NB, NB, NHEAD])
                        TT(dexp[:, 0, :, :], idb, spt[0:NB, 32:48].unsqueeze(1).to_broadcast([NB, NB, NHEAD]), ALU.mult)
                        TT(dexp[:, 1, :, :], idb, sp4[0:NB, 0:NHEAD].unsqueeze(1).to_broadcast([NB, NB, NHEAD]),
                           ALU.mult).then_inc(dexp_ready, 1)
                    if u == 6:
                        dve.wait_ge(samp_spread, 1)
                        for a, dst in ((0, dts_f), (1, dcs_f)):
                            v = b6[:, a * P:(a + 1) * P].rearrange("p (b t q) -> p t b q", b=NB, q=2)
                            last = halves(dst, lambda q: v[64 * q:64 * q + 64, :, :, q])
                        last.then_inc(samp_placed, 1)
                if kind in ("lru", "z"):
                    r = u + (16 if kind == "z" else 0)
                    if r == 0:
                        dve.wait_ge(xbc_ready, 6)
                        make_diag(0)
                        dve.wait_ge(samp_placed, 1)
                        TT(xsdt[:, :, :], xbc[:, 0:KW, NT:COLS], dts_f[:, :, :], ALU.mult).then_inc(samp_placed, 1)
                        make_diag(1)
                    if r == 1:
                        prep(0)
                    if kind == "lru" and j == 3 and t < 3:
                        make_diag(2 * t + 2)
                    if kind == "lru" and j == 0 and t:
                        make_diag(2 * t + 1)
                    if 4 <= r <= 11:
                        item_decay(r - 4)
                    if 15 <= r <= 22:
                        item_decay(r - 7)
                    if 5 <= r <= 12:
                        item_y(r - 5)
                    if 16 <= r <= 23:
                        item_y(r - 8)
                    if 4 <= r <= 11:
                        item_m(r - 4)
                    if 15 <= r <= 22:
                        item_m(r - 7)
                    if r == 13:
                        prep(1)
                    if r == 14:
                        dve.wait_ge(st_made, 3)
                        dve.wait_ge(st_placed, 4)
                        ch.link(TT(s0[:, :, :], s0[:, :, :], cdf[:, :].unsqueeze(2).to_broadcast([P, KW, P]), ALU.mult))
                        TT(s0[:, 0:4, :], s0[:, 0:4, :], b5[:, :].rearrange("p (t n) -> p t n", n=P), ALU.add)
                        TT(s0[:, 4:8, :], s0[:, 4:8, :], b6[:, :].rearrange("p (t n) -> p t n", n=P),
                           ALU.add).then_inc(prep_done, 1)
                if kind == "lru" and j == 1:
                    conv_taps(6 + t)
                if (kind == "lru" and t) or kind == "z":
                    q = t - 1 if kind == "lru" else 3
                    if j == 0 and (kind == "lru" or t == 0):
                        dve.wait_ge(gl_tanh, q + 1)
                        STT(gel[:, :, :], gel[:, :, :], 1.0, main[:, 2:4, 0:COLS], ALU.add,
                            ALU.mult).then_inc(drained[1], 1)
                    if j == 1 and (kind == "lru" or t == 0):
                        dve.wait_ge(drive_ready, q + 1)
                        for h in range(2):
                            ch.add(dve.tensor_tensor_scan(rec[:, h, 0:NT], aa[:, h, 0:NT], th[:, 0, h, 0:NT],
                                                          0.0, ALU.mult, ALU.subtract))
                        h0v = smallcol("state_lru_h", NB * KW).rearrange("p (b t) -> p t b", t=KW)[:, 2 * q:2 * q + 2, :]
                        ch.link(TT(rec[:, :, NT:COLS], aa[:, :, NT:COLS], h0v, ALU.mult))
                        TT(rec[:, :, NT:COLS], rec[:, :, NT:COLS], th[:, 0, :, NT:COLS], ALU.subtract).then_inc(hl_ready, 1)
                        dve.wait_ge(hl_ready, q + 1)
                        dve.wait_ge(drained[1], DRAIN_GL + q + 1)
                        STT(out_l[:, 2 * q:2 * q + 2, :], gel[:, :, :], 0.5, rec[:, :, :], ALU.mult,
                            ALU.mult).then_inc(out_l_ready, 1)
                if kind == "lru" and u or kind == "z" and u == 0:
                    sum_item(u - 1 if kind == "lru" else 15)
                if kind == "lru" and j == 3:
                    dve.wait_ge(decay_tanh, 2 * t + 2)
                    if t:
                        dve.wait_ge(h_captured, t)
                        dve.wait_ge(out_l_ready, t)
                    ch.link(TS(rec[:, :, :], th[:, 0, :, :], -1.0, -1.0, ALU.mult, ALU.add))
                    ch.link(dve.reciprocal(rec[:, :, :], rec[:, :, :]))
                    STT(aa[:, :, :], th[:, 0, :, :], 1.0, rec[:, :, :], ALU.subtract, ALU.mult).then_inc(rec_ready, 1)
                    dve.wait_ge(gl_square, t + 1)
                    ch.link(TS(gel[:, :, :], gel[:, :, :], 0.044715, 1.0, ALU.mult, ALU.add))
                    TT(gel[:, :, :], gel[:, :, :], main[:, 2:4, 0:COLS], ALU.mult).then_inc(gl_inner, 1)
                if kind == "z" and j in (1, 3):
                    p_, par = 2 * t + j // 2, j // 2
                    if p_ == 0:
                        dve.wait_ge(sumsq_spread, 2)
                        ch.link(dve.memset(sumsq[:, :, :], 0.0))
                    dve.wait_ge(drained[par], (e_, o_)[par] + 1)
                    dve.wait_ge(y_placed, 8 + 2 * p_ + 2)
                    v = xbc[:, 2 * p_:2 * p_ + 2, 0:NT]
                    dve.tensor_copy(zs[:, 2 * p_:2 * p_ + 2, :], silu_g[:, :, NT:COLS])
                    TT(v, v, silu_g[:, :, 0:NT], ALU.mult).then_inc(sz_ready, 1)
                    dve.wait_ge(sz_ready, p_ + 1)
                    ch.link(TT(part2[:, :, 0:NT], v, v, ALU.mult))
                    ch.link(TT(sumsq[:, :, 0:NT], sumsq[:, :, 0:NT], part2[:, :, 0:NT], ALU.add))
                if kind == "z" and u == 7:
                    dve.wait_ge(st_sum, 16)
                    ys = xbc[:, 0:KW, NT:COLS]
                    ch.link(TT(ys, ys, dfeat[:, :].unsqueeze(2).to_broadcast([P, KW, NB]), ALU.mult))
                    ch.link(TT(ys, ys, samp[:, 0:KW, :], ALU.add))
                    ch.link(TT(ys, ys, zs[:, :, :], ALU.mult))
                    ch.link(TT(samp[:, 0:KW, :], ys, ys, ALU.mult))
                    dve.tensor_reduce(sumsq[:, 0, NT:COLS], samp[:, 0:KW, :].rearrange("p t b -> p b t"),
                                      AX_X, ALU.add).then_inc(sumsq_ready, 1)
                    for k in range(KW):
                        dve.wait_ge(hhi_ready, 2 * 17 + k + 1)
                        TT(h_lo[:, k, :], out_l[:, k, :], h_hi[:, k, :].bitcast(F32), ALU.subtract).then_inc(h_ready, 1)
                    dve.wait_ge(std_ready, 3)
                    ch.link(dve.reciprocal(rstd[:, :], rstd[:, :]))
                    for k in range(KW + 1):
                        if k < KW:
                            STT(xbc[:, k, :], xbc[:, k, :], smallcol("ssd_norm_g", 1, k), rstd[:, :],
                                ALU.mult, ALU.mult).then_inc(aff_ready, 1)
                        if k:
                            dve.wait_ge(hhi_ready, 2 * 17 + KW + k)
                            TT(h_lo[:, KW + k - 1, :], xbc[:, k - 1, :], h_hi[:, KW + k - 1, :].bitcast(F32),
                               ALU.subtract).then_inc(h_ready, 1)
                    make_gate(G2, 1.0)
                    ch.link(dve.memset(sumsq[:, :, :], 0.0))
                if kind == "out" and j in (1, 3):
                    par = j // 2
                    add_branch(8 * (S_OUT + t) + (8 if par else 4), par, (e_, o_)[par], 2 * (2 * t + par), True)
                if kind == "out" and u == 15:
                    dve.memset(part2[:, 0, 0:1], 0.0).then_inc(sumsq_ready, 1)
                    make_gain(SC3, "g_ffn2")
                    norm(4, SH3, 2 * 17 + KD, 3 * KD)

            for n, seg in enumerate(plan):
                kind, s_first, count, per, vec0, _, _, what = seg
                nxt = last_kind(n)
                squares = kind == "down" and what[1] == NCHUNK - 1
                if kind == "down" and what[2] == 0 and what[1] == 0:
                    make_gate(G1 if what[0] == 0 else G3, 0.5)
                if squares and (n == 0 or plan[n - 1][0] == "up"):
                    ch.link(dve.memset(sumsq[:, :, :], 0.0))
                if kind == "down" and plan[n - 1][0] == "up":
                    dve.wait_ge(act_ready, NCHUNK * UPS * what[0] + UPS * (what[1] + 1))
                if kind == "up" and what == (1, 0, 0):
                    for i in range(4):
                        dve.wait_ge(st_out[i], 16 * 4)
                    dve.wait_ge(stored, 16 * (len(OUT_COPIES) + 1))
                links = per * (1 if kind == "up" else 4 if squares else 2)
                for i, last in turns(dve, seg, peel_first=n == 0, peel_last=differs(n), chain=ch, links=links):
                    for k in range(per):
                        s, e_, o_, par = at_step(seg, i, k)
                        follows = nxt if last and k == per - 1 else PIECE_KIND[kind]
                        for j in range(4):
                            pieces_ahead(s, j, PIECE_KIND[kind], follows)
                            if kind == "up" and j == 3:
                                f, c, at = what
                                pair = i * per + (at + k)
                                done = i * per + (at + k + NCHUNK * UPS * f + UPS * c)
                                dve.wait_ge(piece_used, s * 8 + 8)
                                dve.wait_ge(drained[0], e_ + 1)
                                dve.wait_ge(act_ready, done)
                                TT(part[:, :, :], silu_g[:, :, :], main[:, 2:4, 0:COLS],
                                   ALU.mult).then_inc(drained[1], 1)
                                dve.wait_ge(drained[1], o_ + 1)
                                hi = act_hi[:, bass.ds(pair * 2, 2), :]
                                ch.link(TS(hi, part[:, :, :], 1.0, None, ALU.mult))
                                TT(act_lo[:, bass.ds(pair * 2, 2), :], part[:, :, :], hi.bitcast(F32),
                                   ALU.subtract).then_inc(act_ready, 1)
                            if kind == "down" and j == 3:
                                n0 = i * (2 * per) + 2 * (what[2] + k)
                                add_branch(s * 8 + 8, par, (e_, o_)[par], n0, squares)
                            if kind not in ("up", "down"):
                                dve_tasks(kind, what or 0, j, s, o_, e_)
                    if vec0 is not None:
                        mod_place(i + vec0)
                if kind == "down" and squares and (n + 1 == len(plan) or plan[n + 1][0] != "down"):
                    dve.memset(part2[:, 0, 0:1], 0.0).then_inc(sumsq_ready, 1)
                    if what[0] == 0:
                        make_gain(SC2, "g_mix")
                        norm(2, SH2, 17, KD)
            make_gain(SCF, "g_final")
            norm_samples(5, SHF)
            ysamp = part[:, 0, 0:P].rearrange("p (b k) -> p k b", k=KD)
            TT(ysamp, samp[:, :, :], mods[:, SHF, :, 1:9], ALU.add).then_inc(aff_ready, 1)

            def y_odd(q):
                dve.wait_ge(y_turned, q + 1)
                dve.tensor_copy(yrows[:, :, q * PAIR:(q + 1) * PAIR],
                                main[:, q % 4, :].rearrange("p (c n) -> p c n", c=2)).then_inc(y_rows_odd, 1)
            for k in range(KD):
                if k >= 4:
                    dve.wait_ge(y_turned, (k - 4) // 2 + 1)
                mark = ch.add(TT(ntile[:, k % 4, :], x[:, k, 0:NT], rstd[:, 0:NT], ALU.mult))
                if k % 4 == 2 and k >= 6:
                    y_odd(k // 2 - 2)
                ch.wait(mark)
                TS(ntile[:, k % 4, :], ntile[:, k % 4, :], gain[:, k, 0:1], mods[:, SHF, k, 0:1],
                   ALU.mult, ALU.add).then_inc(aff_ready, 1)
            y_odd(7)

        @block.tensor
        def _(pe):
            MM = nc.tensor.matmul

            def turn(out, src, rows=P):
                return MM(out, src, ident[0:rows, 0:rows], start=True, stop=True)

            def ada_product(vec, k):
                pe.wait_ge(ada_landed[k % 2], vec * (8 * 16) + 16 * (k // 2 + 1))
                if k == 0:
                    if isinstance(vec, int) and vec == 0:
                        pe.wait_ge(c_ready, 1)
                    else:
                        pe.wait_ge(mod_ready, vec)
                for j in range(4):
                    last = MM(b4[32 * j:32 * j + 32, :], cT[:, k, :], ada[:, k % 2, j * 512:(j + 1) * 512],
                              start=k == 0, stop=k == KD - 1, tile_position=(0, 32 * j))
                last.then_inc(ada_used, 1)

            def ada_turn(vec):
                pe.wait_ge(ada_copied, vec + 1)
                for q in range(4):
                    last = turn(b4[:, q * P:(q + 1) * P], ada_sum[:, q * P:(q + 1) * P])
                last.then_inc(ada_turned, 1)

            def sumsq_total(n):
                pe.wait_ge(sumsq_ready, n)
                MM(b6[:, 0:COLS], ones[:, :], sumsq[:, 0, :], start=True, stop=False)
                MM(b6[:, 0:COLS], ones[:, :], sumsq[:, 1, :], start=False, stop=True).then_inc(sumsq_spread, 1)

            def piece(s, m, kind, par, h_base=None, act_base=None, before=None, in_act=False):
                pe.wait_ge(lo_done, s * 8 + (m + 1))
                if before is not None and not (isinstance(before, int) and before == 0):
                    pe.wait_ge(drained[par], before)
                wide = WIDE[kind]
                group = PIECES[kind] if kind != "full" else PIECES[kind][4 * (m // 4):4 * (m // 4) + 4]
                at = sum(group[:m % 4 if kind == "full" else m])
                total = sum(group)
                for kk in range(PIECES[kind][m]):
                    k = at + kk
                    if h_base is not None:
                        pe.wait_ge(h_ready, h_base + k + 1)
                    if act_base is not None and (k % 2 == 0 or kk == 0):
                        pe.wait_ge(act_ready, act_base + k // 2 + 1)
                    hi, lo = (act_hi, act_lo) if in_act else (h_hi, h_lo)
                    for half in range(wide // P):
                        cols = slice(kk * wide + half * P, kk * wide + half * P + P)
                        out = main[:, 2 * par + half, 0:COLS]
                        wh, wl = w_hi[:, m % 4, cols], w_lo[:, m % 4, cols]
                        MM(out, wh, hi[:, k, :], start=k == 0, stop=False)
                        MM(out, wh, lo[:, k, :], start=False, stop=False)
                        last = MM(out, wl, hi[:, k, :], start=False, stop=k == total - 1)
                last.then_inc(piece_used, 1)

            def rows_batch(b):
                bank = (b5, b6)[b % 2]
                if b >= 2:
                    pe.wait_ge(rows_placed, b - 1)
                if b == 0:
                    pe.wait_ge(consts_ready, 1)
                    pe.wait_ge(c_rows, 16 * len([c for c in ROW_COPIES if c[2] < C_TILES]))
                    for tile in range(C_TILES):
                        last = turn(bank[:, tile * P:(tile + 1) * P], rowbuf[:, tile, :])
                elif b <= N_ROWB:
                    pe.wait_ge(other_rows, OTHER_ROWS)
                    for n, tile in enumerate(range(C_TILES + 4 * (b - 1), min(C_TILES + 4 * b, ROW_TILES))):
                        rows = min(P, ROWS - tile * P)
                        last = turn(bank[:, n * P:n * P + rows], rowbuf[0:rows, tile, :], rows)
                else:
                    pe.wait_ge(x_rows, 32)
                    k = 2 * (b - 1 - N_ROWB)
                    for kk in range(2):
                        for c in range(2):
                            last = turn(bank[:, kk * NT + c * P:kk * NT + (c + 1) * P],
                                        xrows[:, c, (k + kk) * P:(k + kk + 1) * P])
                last.then_inc(rows_turned, 1)

            rows_batch(0)
            batches = 1 + N_ROWB + KD // 2
            for k in range(KD):
                ada_product(SH1, k)
                if 2 <= k < 2 + batches - 1:
                    rows_batch(k - 1)
                if k == 2 + batches - 1:
                    MM(b7[:, 0:3 * NHEAD], ones[0:1, :], heads_row[0:1, :], start=True, stop=True).then_inc(heads_spread, 1)
            ada_turn(SH1)
            for k in range(KD):
                ada_product(SC1, k)
            sumsq_total(1)
            ada_turn(SC1)

            def prep(c):
                cs = slice(c * P, (c + 1) * P)
                if c == 0:
                    pe.wait_ge(xbc_ready, 6)
                    pe.wait_ge(samp_placed, 1)
                else:
                    pe.wait_ge(y_placed, 8)
                    pe.wait_ge(gate_taken, 12)
                for g in range(2):
                    turn(b4[:, g * P:(g + 1) * P], xbc[:, 8 + g, cs])
                    MM(b4[:, (2 + g) * P:(3 + g) * P], xbc[:, 8 + g, cs], xbc[:, 10 + g, cs], start=True, stop=True)
                for t in range(KW):
                    last = turn((b5, b6)[t // 4][:, (t % 4) * P:(t % 4 + 1) * P], xbc[:, t, cs])
                last.then_inc(prep_turned, 1)

            def states(c):
                pe.wait_ge(prep_done, c + 1)
                pe.wait_ge(st_placed, 2 + 2 * c)
                for t in range(KW):
                    last = MM((b5, b6)[t // 4][:, (t % 4) * P:(t % 4 + 1) * P], xdec[:, t * P:(t + 1) * P],
                              btok[:, t // 4, :], start=True, stop=True)
                last.then_inc(st_made, 1)

            def states_turned():
                pe.wait_ge(prep_done, 1)
                for g in range(2):
                    last = MM((b5, b6)[g][:, :], btok[:, g, :], xdec[:, g * 512:(g + 1) * 512], start=True, stop=True)
                last.then_inc(st_made, 1)

            def bcast(k):
                c, t = k // 8, k % 8
                if k == 0:
                    pe.wait_ge(st_placed, 4)
                else:
                    pe.wait_ge(d_ready, k)
                if k == 8:
                    pe.wait_ge(prep_done, 3)
                if k > 8:
                    pe.wait_ge(cexp_raw, k - 8)
                for j in range(2):
                    h = 2 * t + j
                    last = MM(b5[:, j * P:(j + 1) * P], dA[:, c, h:h + 1].to_broadcast([P, P]), tri[:, :],
                              start=True, stop=True)
                last.then_inc(bc_made, 1)

            def y_item(k):
                c, t = k // 8, k % 8
                pe.wait_ge(m_ready, k + 1)
                if k:
                    pe.wait_ge(y_placed, k)
                for j in range(2):
                    h = 2 * t + j
                    out = b6[64 * j:64 * j + 64, 0:P]
                    last = MM(out, xdt[:, 64 * h:64 * h + 64], dmat[:, k % 2, j, :], start=True, stop=c == 0)
                    if c:
                        last = MM(out, s0t[:, 64 * h:64 * h + 64], cexp[:, j, :], start=False, stop=True)
                last.then_inc(y_made, 1)

            def diag_sum(n):
                pe.wait_ge(diag_ready, n + 1)
                if n:
                    pe.wait_ge(spread_done, n)
                if n % 2 == 0 and n:
                    pe.wait_ge(gate_taken, 2 * n)
                MM(b7[:, :], ones[:, :], diag.rearrange("p b n -> p (b n)"), start=True, stop=True).then_inc(diag_spread, 1)

            def gates(t):
                pe.wait_ge(gates_in, 64)
                pe.wait_ge(conv_ready, 12 + 2 * (t // 2) + 2)
                if t:
                    pe.wait_ge(gate_taken, 2 * t)
                if t % 2 == 0:
                    pe.wait_ge(spread_done, t + 2)
                if t == 0:
                    pe.wait_ge(prep_done, 1)
                if t == 6:
                    pe.wait_ge(prep_done, 2)
                MM(b4[:, 0:COLS], gates_w[:, 0, t, :], cval[:, t % 2, :], start=True, stop=True)
                MM(b7[:, 0:COLS], gates_w[:, 1, t, :], cval[:, t % 2, :], start=True, stop=True).then_inc(gate_made, 1)

            def pe_tasks(kind, t, j, e_):
                u = 4 * t + j
                if kind == "xbc":
                    if u == 0:
                        pe.wait_ge(drained[0], E_MIX_FIRST)
                        pe.wait_ge(std_ready, 2)
                        turn(b6[:, 0:P], dtq[:, 0:P])
                        turn(b6[:, P:2 * P], dtq[:, P:2 * P])
                        turn(b6[0:NB, 2 * P:3 * P], dtq[:, 2 * P:2 * P + NB], P).then_inc(dt_turned, 1)
                    if u == 3:
                        pe.wait_ge(dA_ready, 1)
                        both = dA[:, 0:2, :].rearrange("p c h -> p (c h)")
                        MM(b7[:, 0:32], tri[:, :], both, start=True, stop=True)
                        MM(b7[:, 32:64], ones[:, :], both, start=True, stop=True).then_inc(cs_spread, 1)
                    if u == 6:
                        pe.wait_ge(dexp_ready, 1)
                        MM(b6[:, 0:2 * P].rearrange("p (a n) -> p a n", a=2), ones[0:NB, :],
                           sumsq[0:NB, :, 0:P], start=True, stop=True).then_inc(samp_spread, 1)
                if kind in ("lru", "z"):
                    r = u + (16 if kind == "z" else 0)
                    if r == 0:
                        prep(0)
                    if r == 2:
                        states_turned()
                    if r == 3:
                        states(0)
                    if 5 <= r <= 12:
                        y_item(r - 5)
                    if 16 <= r <= 23:
                        y_item(r - 8)
                    if 4 <= r <= 11:
                        bcast(r - 4)
                    if r == 13:
                        prep(1)
                    if r == 14:
                        states(1)
                    if 15 <= r <= 22:
                        bcast(r - 7)
                if kind == "lru":
                    if j < 2:
                        diag_sum(2 * t + j)
                    else:
                        gates(2 * t + j - 2)
                if kind == "z" and u == 7:
                    pe.wait_ge(y_placed, 16)
                    sumsq_total(3)
                if kind == "out" and u == 0:
                    pe.wait_ge(captured, 10)
                    pe.wait_ge(h_captured, 4)
                    for tile in range(OUT_TILES):
                        bank = (b5, b6)[tile // 4]
                        if tile == 4:
                            pe.wait_ge(std_ready, 3)
                        last = turn(bank[:, (tile % 4) * P:(tile % 4 + 1) * P], outcol[:, tile * P:(tile + 1) * P])
                        if tile == 3 or tile == OUT_TILES - 1:
                            last.then_inc(out_turned, 1)
                if kind == "out" and u == 15:
                    pe.wait_ge(out_rows_ready, 1)
                    sumsq_total(4)

            for n, seg in enumerate(plan):
                kind, s_first, count, per, vec0, _, _, what = seg
                pk = PIECE_KIND[kind]
                h_base, act_base = None, None
                if kind == "up" and what[1:] == (0, 0):
                    h_base = (0, 3 * KD)[what[0]]
                if kind == "dt":
                    h_base = KD
                if kind == "out" and what == 0:
                    h_base = 2 * KD
                if kind == "down" and what[2] == 0:
                    act_base = NCHUNK * UPS * what[0] + UPS * what[1]
                for i, last in turns(pe, seg, peel_first=n == 0):
                    for k in range(per):
                        s, e_, o_, par = at_step(seg, i, k)
                        for j in range(4):
                            if vec0 is not None:
                                ada_product(i + vec0, 4 * k + j)
                            for m in (2 * j, 2 * j + 1):
                                if pk == "full":
                                    par_m, first = m // 4, m % 4 == 0
                                else:
                                    par_m, first = par, m == 0
                                piece(s, m, pk, par_m, h_base if m < 4 or pk == "dt" else None,
                                      act_base, (e_, o_)[par_m] if first else None, kind == "down")
                            if kind not in ("up", "down"):
                                pe_tasks(kind, what or 0, j, e_)
                    if vec0 is not None:
                        ada_turn(i + vec0)
                if kind == "down" and what[1] == NCHUNK - 1 and (n + 1 == len(plan) or plan[n + 1][0] != "down"):
                    sumsq_total(2 if what[0] == 0 else 5)

            for q in range(KW):
                pe.wait_ge(aff_ready, AFF_FINAL + 2 * q + 2)
                if q >= 4:
                    pe.wait_ge((y_rows_even, y_rows_odd)[q % 2], (q - 4) // 2 + 1)
                for kk in range(2):
                    for c in range(2):
                        last = turn(main[:, q % 4, c * NT + kk * P:c * NT + (kk + 1) * P],
                                    ntile[:, (2 * q + kk) % 4, c * P:(c + 1) * P])
                last.then_inc(y_turned, 1)
            turn(b7[:, 0:P], part[:, 0, 0:P]).then_inc(y_turned, 1)


_INS = ["x_prompt", "x_sample", "c_prompt", "c_sample", "state_lru_h", "state_lru_conv", "state_ssm",
        "state_ssd_conv", "w_ada", "b_ada", "g_ffn1", "w_up1", "w_down1", "g_mix", "w_in", "lru_conv_w",
        "lru_conv_b", "lru_wa", "lru_ba", "lru_wi", "lru_bi", "lru_lambda", "ssd_conv_w", "ssd_conv_b",
        "ssd_dt_bias", "ssd_A_log", "ssd_D", "ssd_norm_g", "w_out", "g_ffn2", "w_up2", "w_down2",
        "w_ada_f", "b_ada_f", "g_final"]
_OUTS = [("y_prompt", (1, NT, D)), ("y_sample", (NB, 1, D)), ("lru_h_prompt", (1, 1, W)),
         ("lru_conv_prompt", (1, 1, CW - 1, W)), ("ssm_prompt", (1, 1, NHEAD, 64, NSTATE)),
         ("ssd_conv_prompt", (1, 1, CW - 1, CONV_C)), ("lru_h_sample", (1, NB, W)),
         ("lru_conv_sample", (1, NB, CW - 1, W)), ("ssm_sample", (1, NB, NHEAD, 64, NSTATE)),
         ("ssd_conv_sample", (1, NB, CW - 1, CONV_C))]


def kernel(**inputs):
    import numpy as _np
    import concourse.bacc as _bacc
    from concourse import mybir as _mybir
    from concourse.bass_utils import run_bass_kernel_spmd as _run

    nc = _bacc.Bacc("TRN2", target_bir_lowering=False, num_devices=1, dynamic_dma_scratch_size=1024)
    arrays, ins, outs = {}, {}, {}
    for name in _INS:
        a = _np.ascontiguousarray(inputs[name])
        arrays[f"in_{name}"] = a
        ins[name] = nc.dram_tensor(f"in_{name}", a.shape, _mybir.dt.from_np(a.dtype), kind="ExternalInput").ap()
    for name, shape in _OUTS:
        outs[name] = nc.dram_tensor(f"out_{name}", shape, _mybir.dt.float32, kind="ExternalOutput").ap()
    build(nc, ins, outs)
    r = _run(nc, [arrays], core_ids=[0])
    return tuple(r.results[0][f"out_{name}"] for name, _ in _OUTS)
```

```python
from contextlib import ExitStack, contextmanager

import concourse.bass as bass
from concourse import mybir

F32 = mybir.dt.float32
F32R = mybir.dt.float32r
ALU = mybir.AluOpType
ACT = mybir.ActivationFunctionType
AX_X = mybir.AxisListType.X

P = 128
D = 2048
KD = D // P
NT = 256
NB = 8
COLS = NT + NB
FF = 5632
KF = FF // P
NCHUNK = 2
KC = KF // NCHUNK
UPS = KC // 2
DNS = KD // 2
W = 1024
KW = W // P
NHEAD = 16
NSTATE = 128
CW = 4
CONV_C = W + 2 * 2 * NSTATE
KX = CONV_C // P
IN_COLS = 2 * W + W + CONV_C + NHEAD
EPS = 1e-6
PAIR = 256
PIECE = 4 * PAIR
CPAD = CW - 1 + NT + NB * CW
COUT = CPAD - (CW - 1)
SAMP0 = CW - 1 + NT

SH1, SC1, G1, SH2, SC2, G2, SH3, SC3, G3, SHF, SCF = range(11)

S_FF1 = 0
S_XBC = S_FF1 + NCHUNK * (UPS + DNS)
S_DT = S_XBC + 1
S_LRU = S_XBC + KX // 4 + 1
S_Z = S_LRU + KW // 2
S_OUT = S_Z + KW // 4
S_FF2 = S_OUT + KD // 4
S_END = S_FF2 + NCHUNK * (UPS + DNS)

Z_SLOTS = (2, 4, 5, 7)
NORM_STEPS = (S_FF1, S_XBC, S_FF2)
PIECES = {
    "full": [4] * 8,
    "down": [3, 3, 3, 3, 3, 3, 2, 2],
    "dt": [2] * 8,
}
WIDE = {"full": PAIR, "down": PAIR, "dt": P}
assert sum(PIECES["down"]) == KC and PIECE >= 4 * PAIR


def blocks_of_rows():
    return [
        ("c_prompt", KD), ("c_sample", NB * KD), ("b_ada", 9 * KD), ("b_ada_f", 2 * KD),
        ("x_sample", NB * KD), ("g_ffn1", KD), ("g_mix", KD), ("g_ffn2", KD), ("g_final", KD),
        ("lru_conv_w", CW * KW), ("lru_conv_b", KW), ("lru_ba", KW), ("lru_bi", KW),
        ("lru_lambda", KW), ("ssd_conv_w", CW * KX), ("ssd_conv_b", KX), ("ssd_norm_g", KW),
        ("state_lru_h", NB * KW), ("state_lru_conv", NB * (CW - 1) * KW),
        ("state_ssd_conv", NB * (CW - 1) * KX),
    ]


def packed(blocks):
    at, copies, row = {}, [], 0
    for name, n in blocks:
        at[name] = row
        done = 0
        while done < n:
            r = (row + done) % P
            m = min(n - done, P - r)
            copies.append((name, done, (row + done) // P, r, m))
            done += m
        row += n
    return at, copies, -(-row // P), row


ROW_AT, ROW_COPIES, ROW_TILES, ROWS = packed(blocks_of_rows())
C_TILES = -(-(9 * KD) // P)
OUT_BLOCKS = [
    ("lru_conv_prompt", (CW - 1) * KW), ("lru_conv_sample", NB * (CW - 1) * KW),
    ("ssd_conv_prompt", (CW - 1) * KX), ("ssd_conv_sample", NB * (CW - 1) * KX),
    ("lru_h_prompt", KW), ("lru_h_sample", NB * KW),
]
N_ROWB = -(-(ROW_TILES - C_TILES) // 4)
OTHER_ROWS = 16 * (len([c for c in ROW_COPIES if c[2] >= C_TILES]) + 3)
OUT_AT, OUT_COPIES, OUT_TILES, OUT_ROWS = packed(OUT_BLOCKS)


class Chain:

    def __init__(self, eng, sem):
        self.eng, self.sem, self.n = eng, sem, 0

    def add(self, ins):
        ins.then_inc(self.sem, 1)
        self.n = self.n + 1
        return self.n

    def wait(self, n=None):
        self.eng.wait_ge(self.sem, self.n if n is None else n)

    def link(self, ins):
        self.add(ins)
        self.wait()

    @contextmanager
    def loop(self, lo, hi, links):
        base = self.n
        with self.eng.Fori(lo, hi) as i:
            self.n = i * links + (base - lo * links)
            yield i
        self.n = base + (hi - lo) * links


def build(nc, ins, outs):
    with ExitStack() as ctx:
        def sb(name, shape, dt=F32):
            return ctx.enter_context(nc.sbuf_tensor(name, shape, dt))

        def sem(name):
            return ctx.enter_context(nc.semaphore(name))

        x = sb("x", [P, KD, COLS])
        h_hi = sb("h_hi", [P, KD, COLS], F32R)
        h_lo = sb("h_lo", [P, KD, COLS], F32R)
        raw = sb("raw", [P, 4, 2 * PIECE])
        w_hi = sb("w_hi", [P, 4, PIECE], F32R)
        w_lo = sb("w_lo", [P, 4, PIECE], F32R)
        small = sb("small", [P, ROW_TILES * P])
        mods = sb("mods", [P, 11, KD, 9])
        gain = sb("gain", [P, KD, 9])
        gate = sb("gate", [P, KD, 9])
        ident = sb("ident", [P, P])
        tri = sb("tri", [P, P])
        ones = sb("ones", [P, P])
        cT = sb("cT", [P, KD, 32])
        eps = sb("eps", [P, 1])
        rstd = sb("rstd", [P, COLS])
        sumsq = sb("sumsq", [P, 2, COLS])
        part = sb("part", [P, 2, COLS])
        part2 = sb("part2", [P, 2, COLS])
        samp = sb("samp", [P, KD, NB])
        silu_g = sb("silu_g", [P, 2, COLS])
        ntile = sb("ntile", [P, 4, NT])
        heads_row = sb("heads_row", [1, 3 * NHEAD])
        heads = sb("heads", [P, 3, NHEAD])
        outcol = sb("outcol", [P, OUT_TILES * P])

        base = nc.sbuf_base
        base = -(-base // 64) * 64
        room = nc.sbuf_usable_end - base

        def layout(entries):
            at, made = base, []
            for name, shape, dt in entries:
                made.append(nc.alloc_sbuf_tensor_at(name, shape, dt, offset=at))
                size = 4
                for n in shape[1:]:
                    size *= n
                at += -(-size // 32) * 32
            assert at <= base + room, (entries[0][0], at - base, room)
            return made

        ada, ada_sum, act_hi, act_lo = layout([
            ("ada", [P, 2, D], F32), ("ada_sum", [P, 512], F32),
            ("act_hi", [P, KC, COLS], F32R), ("act_lo", [P, KC, COLS], F32R)])
        _, _, ada_more, rowbuf, xrows = layout([
            ("ada_s", [P, 2, D], F32), ("ada_sum_s", [P, 512], F32), ("ada_more", [P, 2, D], F32),
            ("rowbuf", [P, ROW_TILES, P], F32), ("xrows", [P, 2, D], F32)])
        _, _, yrows, ysrow = layout([
            ("ada_e", [P, 2, D], F32), ("ada_sum_e", [P, 512], F32),
            ("yrows", [P, 2, D], F32), ("ysrow", [P, P], F32)])
        (xbc, out_l, cin, cfull, cval, xdt, xdec, btok, cbm, s0, s0t, state, spread_b, spread_c,
         gates_w, th, rec, dA, spt, sp2, sp3, sp4, lam2, half_b, exp_a, cst, decl, tot, cdf, dfeat,
         dts_f, dcs_f, xsdt, zs) = layout([
            ("xbc", [P, KX, COLS], F32),
            ("out_l", [P, KW, COLS], F32),
            ("cin", [P, 2, 2, CPAD], F32), ("cfull", [P, 2, COUT], F32),
            ("cval", [P, 2, COLS], F32),
            ("xdt", [P, W], F32), ("xdec", [P, W], F32), ("btok", [P, 2, P], F32),
            ("cbm", [P, 2, P], F32), ("s0", [P, KW, P], F32), ("s0t", [P, W], F32),
            ("state", [P, 4, 4, NSTATE], F32), ("spread_b", [P, 4, NSTATE], F32),
            ("spread_c", [P, 4, NSTATE], F32), ("gates_w", [P, 2, KW, P], F32),
            ("th", [P, 2, 2, COLS], F32), ("rec", [P, 2, COLS], F32),
            ("dA", [P, 3, NHEAD], F32), ("spt", [P, 56], F32),
            ("sp2", [P, 56], F32), ("sp3", [P, 56], F32), ("sp4", [P, 56], F32),
            ("lam2", [P, KW], F32), ("half_b", [P, 2, KW], F32), ("exp_a", [P, NHEAD], F32),
            ("cst", [P, 2, NHEAD], F32), ("decl", [P, 2, NHEAD], F32), ("tot", [P, NHEAD], F32),
            ("cdf", [P, KW], F32), ("dfeat", [P, KW], F32),
            ("dts_f", [P, KW, NB], F32), ("dcs_f", [P, KW, NB], F32), ("xsdt", [P, KW, NB], F32),
            ("zs", [P, KW, NB], F32)])
        diag, prod_even = (ntile[:, 2 * a:2 * a + 2, :].rearrange("p a n -> p (a n)")
                      .rearrange("p (b n) -> p b n", n=NSTATE) for a in (0, 1))
        prod = [prod_even, part2.rearrange("p a n -> p (a n)")[:, 0:512].rearrange("p (b n) -> p b n", n=NSTATE)]
        gel, aa = silu_g, part
        dtq = part2[:, 0, :]
        dexp = sumsq[0:NB, :, 0:P].rearrange("p a (b h) -> p a b h", h=NHEAD)
        outrow = xdt[:, 0:OUT_TILES * P].rearrange("p (a n) -> p a n", n=P)
        dmat = xdec[:, 0:4 * P].rearrange("p (r j n) -> p r j n", r=2, j=2)
        cexp = xdec[:, 4 * P:6 * P].rearrange("p (j n) -> p j n", j=2)

        main = ctx.enter_context(nc.psum_tensor("main", [P, 4, 512], F32))
        b4, b5, b6, b7 = (ctx.enter_context(nc.psum_tensor(f"b{n}", [P, 512], F32))
                          for n in range(4, 8))

        w_landed = [sem(f"w_landed{j}") for j in range(4)]
        ada_landed = [sem(f"ada_landed{j}") for j in range(2)]
        first_landed = [sem(f"first_landed{j}") for j in range(4)]
        hi_done, lo_done = sem("hi_done"), sem("lo_done")
        piece_used = sem("piece_used")
        drained = [sem("drained_even"), sem("drained_odd")]
        ada_used, ada_copied = sem("ada_used"), sem("ada_copied")
        ada_turned, mod_ready = sem("ada_turned"), sem("mod_ready")
        act_ready = sem("act_ready")
        consts_ready = sem("consts_ready")
        c_rows, x_rows, other_rows = sem("c_rows"), sem("x_rows"), sem("other_rows")
        rows_turned, rows_placed, c_ready = sem("rows_turned"), sem("rows_placed"), sem("c_ready")
        heads_spread = sem("heads_spread")
        sumsq_ready, sumsq_spread, std_ready = sem("sumsq_ready"), sem("sumsq_spread"), sem("std_ready")
        aff_ready, hhi_ready, h_ready = sem("aff_ready"), sem("hhi_ready"), sem("h_ready")
        act_chain, dve_chain, pool_chain = sem("act_chain"), sem("dve_chain"), sem("pool_chain")
        dt_turned, cs_spread, dt_exp, dA_ready = sem("dt_turned"), sem("cs_spread"), sem("dt_exp"), sem("dA_ready")
        abs_ready, decl_sub, decl_ready, dexp_ready = sem("abs_ready"), sem("decl_sub"), sem("decl_ready"), sem("dexp_ready")
        samp_spread, samp_placed = sem("samp_spread"), sem("samp_placed")
        mix_init, gates_zero, gates_in = sem("mix_init"), sem("gates_zero"), sem("gates_in")
        hist_ready, captured = sem("hist_ready"), sem("captured")
        conv0_ready, conv_ready, xbc_ready = sem("conv0_ready"), sem("conv_ready"), sem("xbc_ready")
        prep_turned, prep_done = sem("prep_turned"), sem("prep_done")
        st_made, st_placed = sem("st_made"), sem("st_placed")
        bc_made, d_ready, e_ready, cexp_raw, m_ready = (sem(n) for n in (
            "bc_made", "d_ready", "e_ready", "cexp_raw", "m_ready"))
        y_made, y_placed = sem("y_made"), sem("y_placed")
        gate_made, gate_taken, decay_tanh, decay_ready, sqrt_ready, hl_ready, out_l_ready, ix_ready = (
            sem(n) for n in ("gate_made", "gate_taken", "decay_tanh", "decay_ready", "sqrt_ready",
                             "hl_ready", "out_l_ready", "ix_ready"))
        diag_ready, diag_spread, spread_done = sem("diag_ready"), sem("diag_spread"), sem("spread_done")
        st_in = [sem(f"st_in{i}") for i in range(4)]
        st_out = [sem(f"st_out{i}") for i in range(4)]
        st_new, st_prod, st_sum = sem("st_new"), sem("st_prod"), sem("st_sum")
        z_tanh, sz_ready = sem("z_tanh"), sem("sz_ready")
        out_turned, out_rows_ready, stored = sem("out_turned"), sem("out_rows_ready"), sem("stored")
        y_turned = sem("y_turned")
        y_rows_even, y_rows_odd = sem("y_rows_even"), sem("y_rows_odd")
        h_captured, xdt_ready = sem("h_captured"), sem("xdt_ready")

        w_up = [ins[n][0].rearrange("(k p) n -> p k n", p=P) for n in ("w_up1", "w_up2")]
        w_down = [ins[n][0].rearrange("(k p) n -> p k n", p=P) for n in ("w_down1", "w_down2")]
        w_in = ins["w_in"][0].rearrange("(k p) n -> p k n", p=P)
        w_out = ins["w_out"][0].rearrange("(k p) n -> p k n", p=P)
        w_ada = ins["w_ada"][0].rearrange("(k p) n -> p k n", p=P)
        w_ada_f = ins["w_ada_f"].rearrange("(k p) n -> p k n", p=P)
        ssm_in = ins["state_ssm"][0].rearrange("b (t q) p n -> t (q p) b n", q=2)
        ssm_out = outs["ssm_sample"][0].rearrange("b (t q) p n -> t (q p) b n", q=2)

        def rows_of(name):
            a = ins[name]
            flat = {1: "a -> (a)", 2: "a b -> (a b)", 3: "a b c -> (a b c)",
                    4: "a b c d -> (a b c d)"}[len(a.shape)]
            return (a if len(a.shape) == 1 else a.rearrange(flat)).rearrange("(r p) -> r p", p=P)

        def smallcol(name, n, at=0):
            return small[:, ROW_AT[name] + at:ROW_AT[name] + at + n]

        g_of = {n: smallcol(n, KD) for n in ("g_ffn1", "g_mix", "g_ffn2", "g_final")}

        plan = []

        def ffn_plan(f, s, e, o, vec, up_vecs, down_vecs):
            for c in range(NCHUNK):
                n = up_vecs[c]
                plan.append(("up", s, n, 4, vec, e, o, (f, c, 0)))
                plan.append(("up", s + 4 * n, UPS - 4 * n, 1, None, e + 4 * n, o + 4 * n, (f, c, 4 * n)))
                vec += n
                s, e, o = s + UPS, e + UPS, o + UPS
                done = 4 * down_vecs[c]
                if done:
                    plan.append(("down", s, 1, 4, vec, e, o, (f, c, 0)))
                plan.append(("down", s + done, (DNS - done) // 2, 2, None,
                             e + done // 2, o + done // 2, (f, c, done)))
                vec += down_vecs[c]
                s, e, o = s + DNS, e + DNS // 2, o + DNS // 2
            return s, e, o, vec

        s, e, o, vec = ffn_plan(0, 0, 0, 0, 2, (2, 2), (1, 1))
        assert s == S_XBC
        plan.append(("xbc", S_XBC, 1, 1, None, e, o, 0))
        plan.append(("dt", S_DT, 1, 1, None, e + 1, o + 1, None))
        e, o = e + 2, o + 1
        for what, n, first in (("xbc", KX // 4 - 1, S_DT + 1), ("lru", S_Z - S_LRU, S_LRU),
                               ("z", S_OUT - S_Z, S_Z), ("out", S_FF2 - S_OUT, S_OUT)):
            for t in range(n):
                plan.append((what, first + t, 1, 1, None, e, o, t + (what == "xbc")))
                e, o = e + 1, o + 1
        s, e, o, vec = ffn_plan(1, S_FF2, e, o, vec, (1, 2), (0, 0))
        assert s == S_END and vec == 11
        E_DT = [g[5] for g in plan if g[0] == "dt"][0]
        XBC_AT = [(g[1], g[5], g[6]) for g in plan if g[0] == "xbc"]
        Z_AT = [(g[1], g[5], g[6]) for g in plan if g[0] == "z"]
        XL_AT = [(g[1], g[5]) for g in plan if g[0] == "lru"]
        DRAIN_GL = [g[6] for g in plan if g[0] == "lru"][0]
        AFF_FINAL = 2 * (KD + 1) + KW + (KD + 1) + 1
        HHI_FINAL = 2 * (KD + 1) + 2 * KW + (KD + 1)
        PIECE_KIND = {"up": "full", "down": "down", "dt": "dt", "xbc": "full", "lru": "full",
                      "z": "full", "out": "full"}

        def turns(eng, seg, peel_first=False, peel_last=False, chain=None, links=0):
            n = seg[2]
            lo, hi = int(peel_first), n - int(peel_last)
            for i in range(min(lo, n)):
                yield i, i == n - 1
            if hi - lo == 1:
                yield lo, lo == n - 1
            elif hi > lo:
                if chain is None:
                    with eng.Fori(lo, hi) as i:
                        yield i, False
                else:
                    with chain.loop(lo, hi, links) as i:
                        yield i, False
            for i in range(max(hi, lo), n):
                yield i, True

        def at_step(seg, i, k):
            kind, s0_, _, per, _, e0, o0, _ = seg
            s = i * per + (s0_ + k)
            if kind == "down":
                return s, i * (per // 2) + (e0 + (k + 1) // 2), i * (per // 2) + (o0 + k // 2), k % 2
            return s, i * per + (e0 + k), i * per + (o0 + k), 0

        def last_kind(n):
            return PIECE_KIND[plan[n + 1][0]] if n + 1 < len(plan) else None

        def differs(n):
            return last_kind(n) != PIECE_KIND[plan[n][0]]

        def unit_source(seg, i, k, j):
            kind, _, _, per, _, _, _, what = seg
            if kind == "up":
                f, c, at = what
                col = i * (per * PAIR) + ((c * UPS + at + k) * PAIR + (0 if j < 2 else FF))
                return w_up[f][:, 8 * (j % 2):8 * (j % 2) + 8, bass.ds(col, PAIR)]
            if kind == "down":
                f, c, at = what
                k0 = c * KC + sum(PIECES["down"][:2 * j])
                nk = sum(PIECES["down"][2 * j:2 * j + 2])
                return w_down[f][:, k0:k0 + nk, bass.ds(i * (per * PAIR) + (at + k) * PAIR, PAIR)]
            if kind == "dt":
                return w_in[:, 4 * j:4 * j + 4, IN_COLS - P:IN_COLS]
            t, half = what, j // 2
            col = {"xbc": 3 * W + (2 * t + half) * PAIR, "z": 2 * W + (2 * t + half) * PAIR,
                   "lru": t * PAIR + (0 if half == 0 else W), "out": (2 * t + half) * PAIR}[kind]
            w = w_out if kind == "out" else w_in
            return w[:, 8 * (j % 2):8 * (j % 2) + 8, col:col + PAIR]

        def raw_piece(m, kind):
            n, wide = PIECES[kind][m], WIDE[kind]
            first = PIECES[kind][m - 1] if m % 2 else 0
            return raw[:, m // 2, first * wide:(first + n) * wide]

        def split_view(t, m, kind):
            return t[:, m % 4, 0:PIECES[kind][m] * WIDE[kind]]

        def windows(r):
            return cin[:, r, :, SAMP0:SAMP0 + NB * CW].rearrange("p j (b w) -> p j b w", w=CW)

        def pair_of_conv(idx):
            if idx < 6:
                return XBC_AT[idx // 2][0], idx % 2, XBC_AT[idx // 2][1 + idx % 2]
            return XL_AT[idx - 6][0], 0, XL_AT[idx - 6][1]

        def cin_filled(idx):
            _, par, before = pair_of_conv(idx)
            return drained[par], before + 1

        def conv_params(idx, j):
            if idx < 6:
                t = 2 * idx + j
                return (lambda w: smallcol("ssd_conv_w", 1, w * KX + t)), smallcol("ssd_conv_b", 1, t)
            t = 2 * (idx - 6) + j
            return (lambda w: smallcol("lru_conv_w", 1, w * KW + t)), smallcol("lru_conv_b", 1, t)

        def row_copies(eng, of_c, landed):
            for name, r, tile, at, m in ROW_COPIES:
                if (tile < C_TILES) == of_c:
                    eng.dma_start(rowbuf[at:at + m, tile, :], rows_of(name)[r:r + m, :]).then_inc(landed, 16)

        def item_place(n):
            q, i = n // 4, n % 4
            return 4 * (q // 2) + i, slice(4 * (q % 2), 4 * (q % 2) + 4)

        block = ctx.enter_context(nc.Block())

        @block.sync
        def _(sp):
            def ada_load(a, vec, k):
                if not isinstance(a, int) or a >= 2:
                    sp.wait_ge(ada_used, a - 1)
                if isinstance(vec, int) and vec >= SHF:
                    src = w_ada_f[:, k, (vec - SHF) * D:(vec - SHF + 1) * D]
                elif isinstance(vec, int):
                    src = w_ada[:, k, vec * D:(vec + 1) * D]
                else:
                    src = w_ada[:, k, bass.ds(vec * D, D)]
                sp.dma_start(ada[:, k % 2, :], src).then_inc(ada_landed[k % 2], 16)

            row_copies(sp, True, c_rows)
            for a in range(2 * KD):
                if a >= 4:
                    sp.wait_ge(ada_used, a - 3)
                dst = (ada, ada_more)[(a // 2) % 2][:, a % 2, :]
                sp.dma_start(dst, w_ada[:, a % KD, bass.ds(a // KD * D, D)]).then_inc(first_landed[a % 4], 16)
            for n, seg in enumerate(plan):
                kind, s_first, _, per, vec0, _, _, what = seg
                dynamic_f = vec0 is not None and vec0 >= SHF
                for i, _ in turns(sp, seg, peel_first=s_first == 0 or dynamic_f, peel_last=dynamic_f):
                    for k in range(per):
                        s = at_step(seg, i, k)[0]
                        for j in range(4):
                            if not isinstance(s, int) or s >= 1:
                                sp.wait_ge(lo_done, s * 8 + (2 * j - 6))
                            wide = WIDE[PIECE_KIND[kind]]
                            nk = sum(PIECES[PIECE_KIND[kind]][2 * j:2 * j + 2])
                            dst = raw[:, j, 0:nk * wide].rearrange("p (k n) -> p k n", n=wide)
                            sp.dma_start(dst, unit_source(seg, i, k, j)).then_inc(w_landed[j], 16)
                            if vec0 is not None:
                                vec = i + vec0
                                if j == 0 and k == 0 and what[0] == 1 and what[2] == 0:
                                    sp.wait_ge(h_ready, 3 * KD)
                                ada_load(vec * KD + 4 * k + j, vec, 4 * k + j)
            for q in range(4):
                sp.wait_ge(y_rows_even, q + 1)
                sp.wait_ge(y_rows_odd, q + 1)
                sp.dma_start(outs["y_prompt"][0].rearrange("(c p) n -> p c n", p=P)[:, :, q * 512:(q + 1) * 512],
                             yrows[:, :, q * 512:(q + 1) * 512]).then_inc(stored, 16)
            sp.wait_ge(y_rows_even, 5)
            sp.dma_start(outs["y_sample"].rearrange("b s (t p) -> (b s t) p", p=P),
                         ysrow[:, :]).then_inc(stored, 16)
            for i in range(4):
                sp.wait_ge(st_out[i], 16 * 4)
            sp.wait_ge(stored, 16 * (len(OUT_COPIES) + 1 + 5))

        @block.gpsimd
        def _(pool):
            ch = Chain(pool, pool_chain)
            ch.link(pool.memset(ident[:, :], 0.0))
            ch.link(pool.affine_select(out=ident[:, :], in_=ident[:, :], compare_op=ALU.not_equal,
                                       fill=1.0, base=0, pattern=[[-1, P]], channel_multiplier=1))
            ch.link(pool.memset(ones[:, :], 1.0))
            pool.memset(eps[:, :], EPS)
            pool.memset(cT[:, :, :], 0.0)
            pool.memset(outcol[:, OUT_ROWS:], 0.0)
            pool.affine_select(out=tri[:, :], in_=ones[:, :], compare_op=ALU.is_ge, fill=0.0,
                               base=0, pattern=[[1, P]], channel_multiplier=-1).then_inc(consts_ready, 1)
            pool.wait_ge(piece_used, 8 * S_XBC)
            pool.memset(spt[:, :], 0.0)
            pool.memset(cin[:, :, :, 0:CW - 1], 0.0).then_inc(mix_init, 1)
            pool.memset(gates_w[:, :, :, :], 0.0).then_inc(gates_zero, 1)

            def history(idx):
                name, t, kk = ("state_ssd_conv", 2 * idx, KX) if idx < 6 else \
                    ("state_lru_conv", 2 * (idx - 6), KW)
                if idx >= 2:
                    pool.wait_ge(captured, idx - 1)
                    pool.wait_ge(conv_ready, 2 * (idx - 1))
                src = smallcol(name, NB * 3 * kk).rearrange("p (b w t) -> p t b w", w=3, t=kk)
                for j in range(2):
                    ins_ = pool.tensor_copy(windows(idx % 2)[:, j, :, 0:3], src[:, t + j, :, :])
                ins_.then_inc(hist_ready, 1)

            def capture(idx):
                kk, t, a, b = (KX, 2 * idx, "ssd_conv_prompt", "ssd_conv_sample") if idx < 6 else \
                    (KW, 2 * (idx - 6), "lru_conv_prompt", "lru_conv_sample")
                pool.wait_ge(*cin_filled(idx))
                pool.wait_ge(hist_ready, idx + 1)
                for j in range(2):
                    dst = outcol[:, OUT_AT[a]:OUT_AT[a] + 3 * kk].rearrange("p (w t) -> p t w", t=kk)
                    pool.tensor_copy(dst[:, t + j, :], cin[:, idx % 2, j, NT:NT + 3])
                    dst = outcol[:, OUT_AT[b]:OUT_AT[b] + NB * 3 * kk].rearrange(
                        "p (b w t) -> p t b w", w=3, t=kk)
                    ins_ = pool.tensor_copy(dst[:, t + j, :, :], windows(idx % 2)[:, j, :, 1:4])
                ins_.then_inc(captured, 1)

            history(0)
            history(1)
            for idx in range(6):
                capture(idx)
                history(idx + 2)

            def sample_item(n):
                (q, i), t, bs = (n // 4, n % 4), *item_place(n)
                st, pr = state[:, i, :, :], prod[n % 2]
                pool.wait_ge(st_in[i], 16 * (q + 1))
                ch.link(pool.tensor_tensor(st, st, dcs_f[:, t, bs].unsqueeze(2).to_broadcast([P, 4, NSTATE]), ALU.mult))
                pool.wait_ge(spread_done, 2 * q + 1)
                if n >= 2:
                    pool.wait_ge(st_sum, n - 1)
                ch.link(pool.tensor_tensor(pr, spread_b[:, :, :],
                                           xsdt[:, t, bs].unsqueeze(2).to_broadcast([P, 4, NSTATE]), ALU.mult))
                pool.tensor_tensor(st, st, pr, ALU.add).then_inc(st_new, 1)
                pool.wait_ge(st_new, n + 1)
                pool.wait_ge(spread_done, 2 * q + 2)
                pool.tensor_tensor(pr, st, spread_c[:, :, :], ALU.mult).then_inc(st_prod, 1)

            def capture_h(q):
                pool.wait_ge(hl_ready, q + 1)
                pool.tensor_copy(outcol[:, OUT_AT["lru_h_prompt"] + 2 * q:OUT_AT["lru_h_prompt"] + 2 * q + 2],
                                 rec[:, :, NT - 1])
                dst = outcol[:, OUT_AT["lru_h_sample"]:OUT_AT["lru_h_sample"] + NB * KW].rearrange(
                    "p (b t) -> p t b", t=KW)
                pool.tensor_copy(dst[:, 2 * q:2 * q + 2, :], rec[:, :, NT:COLS]).then_inc(h_captured, 1)

            pool.wait_ge(samp_placed, 2)
            for n in range(16):
                sample_item(n)
                if n % 4 == 1:
                    capture(6 + n // 4)
                    if n // 4 < 2:
                        history(8 + n // 4)
                    if n // 4:
                        capture_h(n // 4 - 1)
            capture_h(3)

        @block.scalar
        def _(act):
            ch = Chain(act, act_chain)
            A = nc.scalar.activation

            def hi_piece(s, m, kind):
                v = s * 8 + m
                act.wait_ge(w_landed[m // 2], s * 16 + 16)
                if not isinstance(v, int) or v >= 4:
                    act.wait_ge(piece_used, v - 3)
                A(split_view(w_hi, m, kind), raw_piece(m, kind), ACT.Copy).then_inc(hi_done, 1)

            def pieces_ahead(s, j, kind, nxt):
                for m in (2 * j + 3, 2 * j + 4):
                    if m == 3 and isinstance(s, int) and s in NORM_STEPS:
                        continue
                    if m < 8:
                        hi_piece(s, m, kind)
                    elif nxt is not None:
                        hi_piece(s + 1, m - 8, nxt)

            def ada_copy(vec):
                act.wait_ge(ada_used, vec * KD + KD)
                A(ada_sum[:, :], b4[:, :], ACT.Copy).then_inc(ada_copied, 1)

            def norm_std(n, width):
                act.wait_ge(sumsq_spread, n)
                A(rstd[:, :], b6[:, 0:COLS], ACT.Sqrt, bias=eps[:, 0:1], scale=1.0 / width).then_inc(std_ready, 1)

            def norm_hi(shift, a0, s, inserts):
                act.wait_ge(aff_ready, a0 + 1)
                A(h_hi[:, :, NT:COLS], samp[:, :, :], ACT.Copy).then_inc(hhi_ready, 1)
                for k in range(KD):
                    act.wait_ge(aff_ready, a0 + 2 + k)
                    A(h_hi[:, k, 0:NT], ntile[:, k % 4, :], ACT.Identity,
                      bias=mods[:, shift, k, 0:1]).then_inc(hhi_ready, 1)
                    if k in inserts:
                        hi_piece(s, inserts[k], "full")

            for c in range(2):
                act.dma_start(xrows[:, c, :], ins["x_prompt"][0, c * P:(c + 1) * P, :]).then_inc(x_rows, 16)
            act.wait_ge(rows_placed, 1)
            act.wait_ge(consts_ready, 1)
            A(cT[:, :, 0:9], small[:, 0:9 * KD].rearrange("p (r k) -> p k r", k=KD), ACT.Silu).then_inc(c_ready, 1)
            row_copies(act, False, other_rows)
            for n, name in enumerate(("ssd_dt_bias", "ssd_A_log", "ssd_D")):
                act.dma_start(heads_row[0:1, n * NHEAD:(n + 1) * NHEAD], ins[name]).then_inc(other_rows, 16)
            ada_copy(SH1)
            ada_copy(SC1)
            norm_std(1, D)
            norm_hi(SH1, 0, S_FF1, {3: 0, 7: 1, 11: 2, 15: 3})

            def conv_first(idx):
                step, par, before = pair_of_conv(idx)
                r = idx % 2
                act.wait_ge(piece_used, 8 * step + (8 if par else 4))
                if idx < 2:
                    act.wait_ge(mix_init, 1)
                else:
                    act.wait_ge(captured, idx - 1)
                    act.wait_ge(conv_ready, 2 * (idx - 1))
                A(cin[:, r, :, CW - 1:SAMP0], main[:, 2 * par:2 * par + 2, 0:NT], ACT.Copy)
                A(windows(r)[:, :, :, CW - 1], main[:, 2 * par:2 * par + 2, NT:COLS], ACT.Copy).then_inc(drained[par], 1)
                act.wait_ge(drained[par], before + 1)
                act.wait_ge(hist_ready, idx + 1)
                if idx:
                    act.wait_ge(conv_ready, 2 * idx)
                for j in range(2):
                    w, b = conv_params(idx, j)
                    A(cfull[:, j, :], cin[:, r, j, 0:COUT], ACT.Identity, bias=b,
                      scale=w(0)).then_inc(conv0_ready, 1)

            def xbc_silu(idx):
                act.wait_ge(conv_ready, 2 * (idx + 1))
                A(xbc[:, 2 * idx:2 * idx + 2, :], cval[:, :, :], ACT.Silu).then_inc(xbc_ready, 1)

            def item_exp(k):
                act.wait_ge(d_ready, k + 1)
                if k >= 8:
                    A(cexp, b5[:, 0:2 * P].rearrange("p (j n) -> p j n", j=2), ACT.Exp).then_inc(cexp_raw, 1)
                A(dmat[:, k % 2, :, :], dmat[:, k % 2, :, :], ACT.Exp).then_inc(e_ready, 1)

            def gate_tanh(t):
                act.wait_ge(gate_made, t + 1)
                if t % 2 == 0 and t:
                    act.wait_ge(hl_ready, t // 2)
                for gt, bank in ((0, b4), (1, b7)):
                    A(th[:, gt, t % 2, :], bank[:, 0:COLS], ACT.Tanh, bias=half_b[:, gt, t:t + 1],
                      scale=0.5).then_inc(gate_taken, 1)

            def state_load(n):
                t, bs = item_place(n)
                if n >= 4:
                    act.wait_ge(st_prod, n - 3)
                    act.wait_ge(st_out[n % 4], 16 * (n // 4))
                act.dma_start(state[:, n % 4, :, :], ssm_in[t][:, bs, :]).then_inc(st_in[n % 4], 16)

            def state_store(n):
                t, bs = item_place(n)
                act.wait_ge(st_new, n + 1)
                act.dma_start(ssm_out[t][:, bs, :], state[:, n % 4, :, :]).then_inc(st_out[n % 4], 16)

            def spread_copy(n, dst):
                act.wait_ge(diag_spread, n + 1)
                if n >= 2:
                    act.wait_ge(st_prod, 4 * (n // 2))
                A(dst.rearrange("p b n -> p (b n)"), b7[:, :], ACT.Copy).then_inc(spread_done, 1)

            def act_tasks(kind, t, j):
                u = 4 * t + j
                if kind == "dt" and j == 3:
                    act.wait_ge(piece_used, 8 * S_DT + 8)
                    A(dtq, main[:, 0, 0:COLS], ACT.Copy).then_inc(drained[0], 1)
                    conv_first(1)
                    act.wait_ge(gates_zero, 1)
                    for gt, name in enumerate(("lru_wa", "lru_wi")):
                        for half in range(2):
                            o64 = 64 * half
                            act.dma_start(gates_w[o64:o64 + 64, gt, :, o64:o64 + 64],
                                          ins[name][0].rearrange("(t q) i j -> q i t j", q=2)[half]).then_inc(gates_in, 16)
                if kind == "xbc":
                    if u == 0:
                        act.wait_ge(mix_init, 1)
                        for n in range(4):
                            state_load(n)
                    if j in (0, 2) and (t or j):
                        xbc_silu(2 * t + j // 2 - 1)
                    if j in (1, 3) and u != 3:
                        conv_first(2 * t + j // 2)
                    if u == 5:
                        act.wait_ge(abs_ready, 1)
                        A(sp3[:, :], sp2[:, :], ACT.Exp, scale=-1.0)
                        A(exp_a[:, :], heads[:, 1, :], ACT.Exp).then_inc(dt_exp, 1)
                    if u == 9:
                        act.wait_ge(decl_sub, 1)
                        A(decl[:, :, :], decl[:, :, :], ACT.Exp)
                        A(tot[:, :], b7[:, 48:64], ACT.Exp)
                        A(sp4[0:NB, 0:NHEAD], dA[0:NB, 2, :], ACT.Exp).then_inc(decl_ready, 1)
                if kind in ("lru", "z"):
                    r = u + (16 if kind == "z" else 0)
                    if r == 0:
                        xbc_silu(5)
                    if 3 <= r <= 14:
                        state_load(r + 1)
                    if 2 <= r <= 17:
                        state_store(r - 2)
                    if r == 2:
                        for g in range(2):
                            act.wait_ge(st_made, 1)
                            A(s0t[:, g * 512:(g + 1) * 512], (b5, b6)[g][:, :], ACT.Copy).then_inc(st_placed, 1)
                    if r == 3:
                        act.wait_ge(st_made, 2)
                        for g in range(2):
                            A(s0[:, 4 * g:4 * g + 4, :], (b5, b6)[g][:, :].rearrange("p (t n) -> p t n", n=P),
                              ACT.Copy).then_inc(st_placed, 1)
                    if 4 <= r <= 11:
                        item_exp(r - 4)
                    if 15 <= r <= 22:
                        item_exp(r - 7)
                if kind == "lru":
                    if j == 1:
                        conv_first(6 + t)
                    if j >= 2:
                        gate_tanh(2 * t + j - 2)
                    if j == 3:
                        act.wait_ge(gate_taken, 4 * (t + 1))
                        for h in range(2):
                            A(th[:, 0, h, :], th[:, 0, h, :], ACT.Tanh, bias=lam2[:, 2 * t + h:2 * t + h + 1],
                              scale=lam2[:, 2 * t + h:2 * t + h + 1]).then_inc(decay_tanh, 1)
                if (kind == "lru" and j == 0 and t) or (kind == "z" and u == 0):
                    q = t - 1 if kind == "lru" else 3
                    act.wait_ge(piece_used, 8 * (S_LRU + q) + 8)
                    if q:
                        act.wait_ge(out_l_ready, q)
                    A(gel[:, :, :], main[:, 2:4, 0:COLS], ACT.Gelu_apprx_tanh).then_inc(drained[1], 1)
                    act.wait_ge(decay_ready, q + 1)
                    A(th[:, 0, :, :], th[:, 0, :, :], ACT.Sqrt).then_inc(sqrt_ready, 1)
                if kind == "lru" and j < 2:
                    spread_copy(2 * t + j, (spread_b, spread_c)[j][:, :, :])
                if kind == "z" and u == 7:
                    act.wait_ge(piece_used, 8 * S_OUT - 2)
                    for k in range(4):
                        A(h_hi[:, k, :], out_l[:, k, :], ACT.Copy).then_inc(hhi_ready, 1)
                if kind == "z" and u in Z_SLOTS:
                    p_ = Z_SLOTS.index(u)
                    par = p_ % 2
                    act.wait_ge(piece_used, 8 * Z_AT[p_ // 2][0] + (8 if par else 4))
                    act.wait_ge(out_l_ready, 4)
                    if p_:
                        act.wait_ge(sz_ready, p_)
                    A(silu_g[:, :, :], main[:, 2 * par:2 * par + 2, 0:COLS], ACT.Tanh, scale=0.5).then_inc(z_tanh, 1)
                if kind == "z" and u == 7:
                    norm_std(3, W)
                    for k in range(4, KW):
                        A(h_hi[:, k, :], out_l[:, k, :], ACT.Copy).then_inc(hhi_ready, 1)
                    act.wait_ge(piece_used, 8 * S_OUT)
                    for k in range(KW):
                        act.wait_ge(aff_ready, 2 * 17 + k + 1)
                        A(h_hi[:, KW + k, :], xbc[:, k, :], ACT.Copy).then_inc(hhi_ready, 1)
                if kind == "out":
                    if u == 2:
                        act.wait_ge(out_turned, 2)
                        A(outrow[:, 0:4, :], b5[:, :].rearrange("p (a n) -> p a n", n=P), ACT.Copy)
                        A(outrow[:, 4, :], b6[:, 0:P], ACT.Copy).then_inc(out_rows_ready, 1)
                        act.wait_ge(out_rows_ready, 1)
                        for name, r, tile, at, m in OUT_COPIES:
                            dst = outs[name].rearrange({3: "a b c -> (a b c)", 4: "a b c d -> (a b c d)"}[
                                len(outs[name].shape)]).rearrange("(r p) -> r p", p=P)
                            act.dma_start(dst[r:r + m, :], outrow[at:at + m, tile, :]).then_inc(stored, 16)
                        act.wait_ge(prep_done, 3)
                        act.dma_start(outs["ssm_prompt"][0, 0].rearrange("(t q) p n -> (q p) t n", q=2),
                                      s0[:, :, :]).then_inc(stored, 16)
                if kind == "out" and u == 15:
                    hi_piece(S_FF2, 3, "full")
                    norm_std(4, D)
                    norm_hi(SH3, 2 * 17 + KW, S_FF2, {})

            for n, seg in enumerate(plan):
                kind, s_first, count, per, vec0, _, _, what = seg
                nxt = last_kind(n)
                for i, last in turns(act, seg, peel_first=n == 0, peel_last=differs(n)):
                    for k in range(per):
                        s, e_, o_, par = at_step(seg, i, k)
                        follows = nxt if last and k == per - 1 else PIECE_KIND[kind]
                        for j in range(4):
                            pieces_ahead(s, j, PIECE_KIND[kind], follows)
                            if kind == "up" and j == 1:
                                act.wait_ge(piece_used, s * 8 + 4)
                                act.wait_ge(drained[1], o_)
                                A(silu_g[:, :, :], main[:, 0:2, 0:COLS], ACT.Silu).then_inc(drained[0], 1)
                            if kind not in ("up", "down"):
                                act_tasks(kind, what or 0, j)
                    if vec0 is not None:
                        ada_copy(i + vec0)
                if kind == "down" and what[0] == 0 and what[1] == 1 and plan[n + 1][0] == "xbc":
                    hi_piece(S_XBC, 3, "full")
                    norm_std(2, D)
                    norm_hi(SH2, 17, S_XBC, {})
            norm_std(5, D)
            for q in range(KW + 2):
                for k in (2 * q, 2 * q + 1):
                    if k < KD:
                        act.wait_ge(aff_ready, AFF_FINAL + k + 1)
                        A(ntile[:, k % 4, :], ntile[:, k % 4, :], ACT.Identity,
                          bias=mods[:, SHF, k, 0:1]).then_inc(hhi_ready, 1)
                q -= 2
                if q < 0 or q % 2:
                    continue
                act.wait_ge(y_turned, q + 1)
                A(yrows[:, :, q * PAIR:(q + 1) * PAIR],
                  main[:, q % 4, :].rearrange("p (c n) -> p c n", c=2), ACT.Copy).then_inc(y_rows_even, 1)
            act.wait_ge(y_turned, KW + 1)
            A(ysrow[:, :], b7[:, 0:P], ACT.Copy).then_inc(y_rows_even, 1)

        @block.vector
        def _(dve):
            ch = Chain(dve, dve_chain)
            TT, TS, STT = dve.tensor_tensor, dve.tensor_scalar, dve.scalar_tensor_tensor

            def lo_piece(s, m, kind):
                v = s * 8 + m
                dve.wait_ge(hi_done, v + 1)
                TT(split_view(w_lo, m, kind), raw_piece(m, kind),
                   split_view(w_hi, m, kind).bitcast(F32), ALU.subtract).then_inc(lo_done, 1)

            def pieces_ahead(s, j, kind, nxt):
                for m in (2 * j + 3, 2 * j + 4):
                    if m == 3 and isinstance(s, int) and s in NORM_STEPS:
                        continue
                    if m == 10 and isinstance(s, int) and s + 1 in NORM_STEPS:
                        continue
                    if m < 8:
                        lo_piece(s, m, kind)
                    elif nxt is not None:
                        lo_piece(s + 1, m - 8, nxt)

            def mod_place(vec):
                dve.wait_ge(ada_turned, vec + 1)
                src = b4[:, :].rearrange("p (q j r) -> p q j r", q=4, j=4)[:, :, :, 0:9]
                dst = mods[:, bass.ds(vec, 1), :, :].rearrange("p a (j q) r -> p (a q) j r", q=4)
                bias = small[:, bass.ds(vec * KD + ROW_AT["b_ada"], KD)].rearrange(
                    "p (j q) -> p q j", q=4).unsqueeze(3).to_broadcast([P, 4, 4, 9])
                for q in range(4):
                    ins_ = TT(dst[:, q, :, :], src[:, q, :, :], bias[:, q, :, :], ALU.add)
                ins_.then_inc(mod_ready, 1)

            def make_gain(vec, name):
                dve.wait_ge(mod_ready, vec + 1)
                ch.link(STT(gain[:, :, :], mods[:, vec, :, :], 1.0,
                            g_of[name].unsqueeze(2).to_broadcast([P, KD, 9]), ALU.add, ALU.mult))

            def make_gate(vec, factor):
                dve.wait_ge(mod_ready, vec + 1)
                ch.link(TS(gate[:, :, :], mods[:, vec, :, :], factor, None, ALU.mult))

            def norm_samples():
                ch.link(TT(samp[:, :, :], x[:, :, NT:COLS],
                           rstd[:, NT:COLS].unsqueeze(1).to_broadcast([P, KD, NB]), ALU.mult))
                ch.link(TT(samp[:, :, :], samp[:, :, :], gain[:, :, 1:9], ALU.mult))

            def norm(n, shift, a0, h0, s, inserts):
                dve.wait_ge(std_ready, n)
                ch.link(dve.reciprocal(rstd[:, :], rstd[:, :]))

                norm_samples()
                TT(samp[:, :, :], samp[:, :, :], mods[:, shift, :, 1:9], ALU.add).then_inc(aff_ready, 1)

                def lo(k):
                    dve.wait_ge(hhi_ready, a0 + 2 + k)
                    STT(h_lo[:, k, 0:NT], ntile[:, k % 4, :], mods[:, shift, k, 0:1],
                        h_hi[:, k, 0:NT].bitcast(F32), ALU.add, ALU.subtract).then_inc(h_ready, 1)
                for k in range(KD):
                    if k >= 4:
                        dve.wait_ge(h_ready, h0 + k - 3)
                    STT(ntile[:, k % 4, :], x[:, k, 0:NT], gain[:, k, 0:1], rstd[:, 0:NT],
                        ALU.mult, ALU.mult).then_inc(aff_ready, 1)
                    if k == 1:
                        dve.wait_ge(hhi_ready, a0 + 1)
                        TT(h_lo[:, :, NT:COLS], samp[:, :, :], h_hi[:, :, NT:COLS].bitcast(F32), ALU.subtract)
                    if k >= 1:
                        lo(k - 1)
                    if k in inserts:
                        lo_piece(s, inserts[k], "full")
                lo(KD - 1)

            def add_branch(s, par, before, n0, squares):
                dve.wait_ge(piece_used, s)
                ps = main[:, 2 * par:2 * par + 2, :]
                for h in range(2):
                    xt = x[:, bass.ds(n0 + h, 1), 0:NT]
                    STT(xt, ps[:, h:h + 1, 0:NT], gate[:, bass.ds(n0 + h, 1), 0:1].rearrange("p a b -> p (a b)"),
                        xt, ALU.mult, ALU.add)
                xs = x[:, bass.ds(n0, 2), :]
                TT(part[:, :, NT:COLS], ps[:, :, NT:COLS], gate[:, bass.ds(n0, 2), 1:9],
                   ALU.mult).then_inc(drained[par], 1)
                dve.wait_ge(drained[par], before + 1)
                ch.link(TT(xs[:, :, NT:COLS], xs[:, :, NT:COLS], part[:, :, NT:COLS], ALU.add))
                if squares:
                    ch.link(TT(part2[:, :, :], xs, xs, ALU.mult))
                    ch.link(TT(sumsq[:, :, :], sumsq[:, :, :], part2[:, :, :], ALU.add))

            def place(b):
                bank = (b5, b6)[b % 2]
                dve.wait_ge(rows_turned, b + 1)
                if b == 0:
                    dve.tensor_copy(small[:, 0:C_TILES * P], bank[:, 0:C_TILES * P]).then_inc(rows_placed, 1)
                elif b > KD // 2:
                    b -= KD // 2
                    lo_r, hi_r = (C_TILES + 4 * (b - 1)) * P, min((C_TILES + 4 * b) * P, ROWS)
                    dve.tensor_copy(small[:, lo_r:hi_r], bank[:, 0:hi_r - lo_r]).then_inc(rows_placed, 1)
                else:
                    k = 2 * (b - 1)
                    dve.tensor_copy(x[:, k:k + 2, 0:NT], bank[:, :].rearrange("p (k n) -> p k n", k=2)).then_inc(rows_placed, 1)
            for b in range(1 + N_ROWB + KD // 2):
                place(b)
            dve.wait_ge(rows_placed, 1 + N_ROWB + KD // 2)
            ch.link(dve.tensor_copy(x[:, :, NT:COLS], smallcol("x_sample", NB * KD).rearrange("p (b k) -> p k b", k=KD)))
            dve.wait_ge(heads_spread, 1)
            ch.link(dve.tensor_copy(heads[:, :, :], b7[:, 0:3 * NHEAD].rearrange("p (a h) -> p a h", a=3)))
            ch.link(dve.memset(sumsq[:, :, :], 0.0))
            for k in range(0, KD, 2):
                ch.link(TT(part2[:, :, :], x[:, k:k + 2, :], x[:, k:k + 2, :], ALU.mult))
                if k < KD - 2:
                    ch.link(TT(sumsq[:, :, :], sumsq[:, :, :], part2[:, :, :], ALU.add))
                else:
                    TT(sumsq[:, :, :], sumsq[:, :, :], part2[:, :, :], ALU.add).then_inc(sumsq_ready, 1)
            mod_place(SH1)
            mod_place(SC1)
            make_gain(SC1, "g_ffn1")
            norm(1, SH1, 0, 0, S_FF1, {3: 0, 7: 1, 11: 2, 15: 3})

            def conv_taps(idx):
                r = idx % 2
                if 0 < idx <= 6:
                    dve.wait_ge(xbc_ready, idx)
                elif idx > 6:
                    dve.wait_ge(ix_ready, idx - 6)
                    dve.wait_ge(gate_made, 2 * (idx - 6))
                for w in (1, 2):
                    for j in range(2):
                        dve.wait_ge(conv0_ready, 2 * idx + j + 1)
                        if w == 2:
                            ch.wait(marks[j])
                        tap, _ = conv_params(idx, j)
                        mark = ch.add(STT(cfull[:, j, :], cin[:, r, j, w:w + COUT], tap(w),
                                          cfull[:, j, :], ALU.mult, ALU.add))
                        marks = [mark] if j == 0 and w == 1 else marks + [mark]
                ch.wait()
                for j in range(2):
                    tap, _ = conv_params(idx, j)
                    STT(cval[:, j, 0:NT], cin[:, r, j, 3:3 + NT], tap(3), cfull[:, j, 0:NT], ALU.mult, ALU.add)
                    win = cfull[:, j, SAMP0 - 0:SAMP0 + 4 * NB - 3:4]
                    STT(cval[:, j, NT:COLS], windows(r)[:, j, :, 3], tap(3), win,
                        ALU.mult, ALU.add).then_inc(conv_ready, 1)

            def halves(dst, src_of):
                for q in range(2):
                    last = dve.tensor_copy(dst[64 * q:64 * q + 64], src_of(q))
                return last

            def prep(c):
                dve.wait_ge(prep_turned, c + 1)
                dve.tensor_copy(btok[:, :, :], b4[:, 0:2 * P].rearrange("p (g n) -> p g n", g=2))
                TT(cbm[:, :, :], b4[:, 2 * P:4 * P].rearrange("p (g n) -> p g n", g=2),
                   tri[:, :].unsqueeze(1).to_broadcast([P, 2, P]), ALU.mult)
                for g in range(2):
                    TT(xdt[:, g * 512:(g + 1) * 512].rearrange("p (h n) -> p h n", n=64),
                       (b5, b6)[g][:, :].rearrange("p (h n) -> p h n", n=64),
                       spt[:, c * NHEAD + 8 * g:c * NHEAD + 8 * g + 8].unsqueeze(2).to_broadcast([P, 8, 64]),
                       ALU.mult).then_inc(xdt_ready, 1)
                dve.wait_ge(xdt_ready, 2 * c + 2)
                TT(xdec[:, :].rearrange("p (h n) -> p h n", n=64), xdt[:, :].rearrange("p (h n) -> p h n", n=64),
                   decl[:, c, :].unsqueeze(2).to_broadcast([P, NHEAD, 64]), ALU.mult).then_inc(prep_done, 1)

            def item_decay(k):
                c, t = k // 8, k % 8
                dve.wait_ge(bc_made, k + 1)
                for j in range(2):
                    ins_ = TS(dmat[:, k % 2, j, :], b5[:, j * P:(j + 1) * P],
                              cst[:, c, 2 * t + j:2 * t + j + 1], 0.0, ALU.subtract, ALU.min)
                ins_.then_inc(d_ready, 1)

            def item_m(k):
                c, t = k // 8, k % 8
                g = t // 4
                if k >= 8:
                    dve.wait_ge(cexp_raw, k - 7)
                    TT(cexp, cexp, xbc[:, 10 + g, c * P:(c + 1) * P].unsqueeze(1).to_broadcast([P, 2, P]), ALU.mult)
                dve.wait_ge(e_ready, k + 1)
                TT(dmat[:, k % 2, :, :], dmat[:, k % 2, :, :],
                   cbm[:, g, :].unsqueeze(1).to_broadcast([P, 2, P]), ALU.mult).then_inc(m_ready, 1)

            def item_y(k):
                c, t = k // 8, k % 8
                dve.wait_ge(y_made, k + 1)
                v = xbc[:, t, c * P:(c + 1) * P]
                STT(v, v, dfeat[:, t:t + 1], b6[:, 0:P], ALU.mult, ALU.add).then_inc(y_placed, 1)

            def make_diag(n):
                q, cc = n // 2, n % 2
                g, half = q // 2, q % 2
                if n:
                    dve.wait_ge(diag_spread, n)
                src = xbc[:, 8 + 2 * cc + g, NT + 4 * half:NT + 4 * half + 4]
                TT(diag, ident[:, :].unsqueeze(1).to_broadcast([P, 4, P]),
                   src.unsqueeze(2).to_broadcast([P, 4, P]), ALU.mult).then_inc(diag_ready, 1)

            def sum_item(n):
                q, i = n // 4, n % 4
                g, half = q // 2, q % 2
                dve.wait_ge(st_prod, n + 1)
                dve.tensor_reduce(samp[:, 4 * g + i, 4 * half:4 * half + 4], prod[n % 2], AX_X, ALU.add).then_inc(st_sum, 1)

            def dve_tasks(kind, t, j, s, o_, e_):
                u = 4 * t + j
                if kind == "dt" and j == 3:
                    conv_taps(1)
                if kind == "xbc":
                    if j in (1, 3) and u != 3:
                        conv_taps(2 * t + j // 2)
                    if u == 4:
                        dve.wait_ge(dt_turned, 1)
                        dve.wait_ge(mix_init, 1)
                        TT(spt[:, 0:32].rearrange("p (c h) -> p c h", c=2),
                           b6[:, 0:2 * P].rearrange("p (c h) -> p c h", c=2)[:, :, P - NHEAD:P],
                           heads[:, 0:1, :].to_broadcast([P, 2, NHEAD]), ALU.add)
                        TT(spt[0:NB, 32:48], b6[0:NB, 3 * P - NHEAD:3 * P], heads[0:NB, 0, :], ALU.add)
                        ch.link(TS(spt[:, 48:56], smallcol("lru_lambda", KW), -1.0, None, ALU.mult))
                        STT(sp2[:, :], spt[:, :], -1.0, spt[:, :], ALU.mult, ALU.max).then_inc(abs_ready, 1)
                    if u == 5:
                        dve.wait_ge(dt_exp, 1)
                        ch.link(TS(sp2[:, :], sp3[:, :], 2.0, None, ALU.add))
                        ch.link(dve.reciprocal(sp2[:, :], sp2[:, :]))
                        ch.link(TT(sp2[:, :], sp2[:, :], sp3[:, :], ALU.mult))
                        ch.link(TT(sp3[:, :], sp2[:, :], sp2[:, :], ALU.mult))
                        ch.link(TS(sp4[:, :], sp3[:, :], 1.0 / 17, None, ALU.mult))
                        for odd in (15, 13, 11, 9, 7, 5, 3):
                            ch.link(STT(sp4[:, :], sp4[:, :], 1.0 / odd, sp3[:, :], ALU.add, ALU.mult))
                        ch.link(STT(sp4[:, :], sp4[:, :], 1.0, sp2[:, :], ALU.add, ALU.mult))
                        ch.link(TS(spt[:, :], spt[:, :], 0.0, None, ALU.max))
                        ch.link(STT(spt[:, :], sp4[:, :], 2.0, spt[:, :], ALU.mult, ALU.add))
                        TS(lam2[:, :], spt[:, 48:56], 2.0, None, ALU.mult)
                        TS(half_b[:, 0, :], smallcol("lru_ba", KW), 0.5, None, ALU.mult)
                        TS(half_b[:, 1, :], smallcol("lru_bi", KW), 0.5, None, ALU.mult)
                        STT(dA[:, :, :], spt[:, 0:48].rearrange("p (c h) -> p c h", c=3), -1.0,
                            exp_a[:, :].unsqueeze(1).to_broadcast([P, 3, NHEAD]), ALU.mult, ALU.mult).then_inc(dA_ready, 1)
                    if u == 8:
                        dve.wait_ge(cs_spread, 1)
                        ch.link(dve.tensor_copy(cst[:, :, :], b7[:, 0:32].rearrange("p (c h) -> p c h", c=2)))
                        TT(decl[:, :, :], b7[:, 32:64].rearrange("p (c h) -> p c h", c=2), cst[:, :, :],
                           ALU.subtract).then_inc(decl_sub, 1)
                    if u == 9:
                        dve.wait_ge(decl_ready, 1)
                        halves(cdf, lambda q: tot[64 * q:64 * q + 64, q:NHEAD:2])
                        halves(dfeat, lambda q: heads[64 * q:64 * q + 64, 2, q:NHEAD:2])
                        idb = ident[0:NB, 0:NB].unsqueeze(2).to_broadcast([NB, NB, NHEAD])
                        TT(dexp[:, 0, :, :], idb, spt[0:NB, 32:48].unsqueeze(1).to_broadcast([NB, NB, NHEAD]), ALU.mult)
                        TT(dexp[:, 1, :, :], idb, sp4[0:NB, 0:NHEAD].unsqueeze(1).to_broadcast([NB, NB, NHEAD]),
                           ALU.mult).then_inc(dexp_ready, 1)
                    if u == 10:
                        dve.wait_ge(samp_spread, 1)
                        for a, dst in ((0, dts_f), (1, dcs_f)):
                            v = b6[:, a * P:(a + 1) * P].rearrange("p (b t q) -> p t b q", b=NB, q=2)
                            last = halves(dst, lambda q: v[64 * q:64 * q + 64, :, :, q])
                        last.then_inc(samp_placed, 1)
                if kind in ("lru", "z"):
                    r = u + (16 if kind == "z" else 0)
                    if r == 0:
                        dve.wait_ge(xbc_ready, 6)
                        make_diag(0)
                        dve.wait_ge(samp_placed, 1)
                        TT(xsdt[:, :, :], xbc[:, 0:KW, NT:COLS], dts_f[:, :, :], ALU.mult).then_inc(samp_placed, 1)
                        make_diag(1)
                    if r == 1:
                        prep(0)
                    if kind == "lru" and j == 3 and t < 3:
                        make_diag(2 * t + 2)
                    if kind == "lru" and j == 0 and t:
                        make_diag(2 * t + 1)
                    if 4 <= r <= 11:
                        item_decay(r - 4)
                    if 15 <= r <= 22:
                        item_decay(r - 7)
                    if 5 <= r <= 12:
                        item_y(r - 5)
                    if 16 <= r <= 23:
                        item_y(r - 8)
                    if 4 <= r <= 11:
                        item_m(r - 4)
                    if 15 <= r <= 22:
                        item_m(r - 7)
                    if r == 13:
                        prep(1)
                    if r == 14:
                        dve.wait_ge(st_made, 3)
                        dve.wait_ge(st_placed, 4)
                        ch.link(TT(s0[:, :, :], s0[:, :, :], cdf[:, :].unsqueeze(2).to_broadcast([P, KW, P]), ALU.mult))
                        TT(s0[:, 0:4, :], s0[:, 0:4, :], b5[:, :].rearrange("p (t n) -> p t n", n=P), ALU.add)
                        TT(s0[:, 4:8, :], s0[:, 4:8, :], b6[:, :].rearrange("p (t n) -> p t n", n=P),
                           ALU.add).then_inc(prep_done, 1)
                if kind == "lru" and j == 1:
                    conv_taps(6 + t)
                if (kind == "lru" and t) or kind == "z":
                    q = t - 1 if kind == "lru" else 3
                    if j == 1 and (kind == "lru" or t == 0):
                        dve.wait_ge(sqrt_ready, q + 1)
                        ch.link(TT(th[:, 0, :, :], th[:, 0, :, :], rec[:, :, :], ALU.mult))
                        ch.link(TT(th[:, 0, :, :], th[:, 0, :, :], th[:, 1, :, :], ALU.mult))
                        for h in range(2):
                            ch.add(dve.tensor_tensor_scan(rec[:, h, 0:NT], aa[:, h, 0:NT], th[:, 0, h, 0:NT],
                                                          0.0, ALU.mult, ALU.add))
                        h0v = smallcol("state_lru_h", NB * KW).rearrange("p (b t) -> p t b", t=KW)[:, 2 * q:2 * q + 2, :]
                        ch.link(TT(rec[:, :, NT:COLS], aa[:, :, NT:COLS], h0v, ALU.mult))
                        TT(rec[:, :, NT:COLS], rec[:, :, NT:COLS], th[:, 0, :, NT:COLS], ALU.add).then_inc(hl_ready, 1)
                        dve.wait_ge(hl_ready, q + 1)
                        dve.wait_ge(drained[1], DRAIN_GL + q + 1)
                        TT(out_l[:, 2 * q:2 * q + 2, :], gel[:, :, :], rec[:, :, :], ALU.mult).then_inc(out_l_ready, 1)
                if kind == "lru" and u or kind == "z" and u == 0:
                    sum_item(u - 1 if kind == "lru" else 15)
                if kind == "lru" and j == 3:
                    dve.wait_ge(decay_tanh, 2 * t + 2)
                    if t:
                        dve.wait_ge(h_captured, t)
                        dve.wait_ge(out_l_ready, t)
                    ch.link(TS(rec[:, :, :], th[:, 0, :, :], 1.0, None, ALU.add))
                    ch.link(dve.reciprocal(rec[:, :, :], rec[:, :, :]))
                    TS(aa[:, :, :], rec[:, :, :], 2.0, -1.0, ALU.mult, ALU.add).then_inc(decay_ready, 1)
                    STT(th[:, 1, :, :], th[:, 1, :, :], 1.0, cval[:, :, :], ALU.add, ALU.mult).then_inc(ix_ready, 1)
                def out_l_lo(k):
                    dve.wait_ge(hhi_ready, 2 * 17 + k + 1)
                    TT(h_lo[:, k, :], out_l[:, k, :], h_hi[:, k, :].bitcast(F32), ALU.subtract).then_inc(h_ready, 1)
                if kind == "z" and u == 7:
                    for k in range(4):
                        out_l_lo(k)
                if kind == "z" and u in Z_SLOTS:
                    p_ = Z_SLOTS.index(u)
                    par = p_ % 2
                    if p_ == 0:
                        dve.wait_ge(sumsq_spread, 2)
                        ch.link(dve.memset(sumsq[:, :, :], 0.0))
                    dve.wait_ge(z_tanh, p_ + 1)
                    STT(silu_g[:, :, :], silu_g[:, :, :], 1.0, main[:, 2 * par:2 * par + 2, 0:COLS],
                        ALU.add, ALU.mult).then_inc(drained[par], 1)
                    dve.wait_ge(drained[par], Z_AT[p_ // 2][1 + par] + 1)
                    dve.wait_ge(y_placed, 8 + 2 * p_ + 2)
                    v = xbc[:, 2 * p_:2 * p_ + 2, 0:NT]
                    dve.tensor_copy(zs[:, 2 * p_:2 * p_ + 2, :], silu_g[:, :, NT:COLS])
                    STT(v, v, 0.5, silu_g[:, :, 0:NT], ALU.mult, ALU.mult).then_inc(sz_ready, 1)
                    dve.wait_ge(sz_ready, p_ + 1)
                    ch.link(TT(part2[:, :, 0:NT], v, v, ALU.mult))
                    ch.link(TT(sumsq[:, :, 0:NT], sumsq[:, :, 0:NT], part2[:, :, 0:NT], ALU.add))
                if kind == "z" and u == 7:
                    dve.wait_ge(st_sum, 16)
                    ys = xbc[:, 0:KW, NT:COLS]
                    ch.link(TT(ys, ys, dfeat[:, :].unsqueeze(2).to_broadcast([P, KW, NB]), ALU.mult))
                    ch.link(TT(ys, ys, samp[:, 0:KW, :], ALU.add))
                    ch.link(STT(ys, ys, 0.5, zs[:, :, :], ALU.mult, ALU.mult))
                    ch.link(TT(samp[:, 0:KW, :], ys, ys, ALU.mult))
                    dve.tensor_reduce(sumsq[:, 0, NT:COLS], samp[:, 0:KW, :].rearrange("p t b -> p b t"),
                                      AX_X, ALU.add).then_inc(sumsq_ready, 1)
                    dve.wait_ge(std_ready, 3)
                    mark = ch.add(dve.reciprocal(rstd[:, :], rstd[:, :]))
                    for k in range(4, KW):
                        out_l_lo(k)
                    ch.wait(mark)
                    for k in range(KW + 1):
                        if k < KW:
                            STT(xbc[:, k, :], xbc[:, k, :], smallcol("ssd_norm_g", 1, k), rstd[:, :],
                                ALU.mult, ALU.mult).then_inc(aff_ready, 1)
                        if k:
                            dve.wait_ge(hhi_ready, 2 * 17 + KW + k)
                            TT(h_lo[:, KW + k - 1, :], xbc[:, k - 1, :], h_hi[:, KW + k - 1, :].bitcast(F32),
                               ALU.subtract).then_inc(h_ready, 1)
                    make_gate(G2, 1.0)
                    ch.link(dve.memset(sumsq[:, :, :], 0.0))
                if kind == "out" and j in (1, 3):
                    par = j // 2
                    add_branch(8 * (S_OUT + t) + (8 if par else 4), par, (e_, o_)[par], 2 * (2 * t + par), True)
                if kind == "out" and u == 15:
                    dve.memset(part2[:, 0, 0:1], 0.0).then_inc(sumsq_ready, 1)
                    lo_piece(S_FF2, 2, "full")
                    lo_piece(S_FF2, 3, "full")
                    make_gain(SC3, "g_ffn2")
                    norm(4, SH3, 2 * 17 + KD, 3 * KD, S_FF2, {})

            for n, seg in enumerate(plan):
                kind, s_first, count, per, vec0, _, _, what = seg
                nxt = last_kind(n)
                squares = kind == "down" and what[1] == NCHUNK - 1
                if kind == "down" and what[2] == 0 and what[1] == 0:
                    make_gate(G1 if what[0] == 0 else G3, 0.5)
                if squares and (n == 0 or plan[n - 1][0] == "up"):
                    ch.link(dve.memset(sumsq[:, :, :], 0.0))
                if kind == "down" and plan[n - 1][0] == "up":
                    dve.wait_ge(act_ready, NCHUNK * UPS * what[0] + UPS * (what[1] + 1))
                if kind == "up" and what == (1, 0, 0):
                    for i in range(4):
                        dve.wait_ge(st_out[i], 16 * 4)
                    dve.wait_ge(stored, 16 * (len(OUT_COPIES) + 1))
                links = per * (1 if kind == "up" else 3 if squares else 1)
                for i, last in turns(dve, seg, peel_first=n == 0, peel_last=differs(n), chain=ch, links=links):
                    for k in range(per):
                        s, e_, o_, par = at_step(seg, i, k)
                        follows = nxt if last and k == per - 1 else PIECE_KIND[kind]
                        for j in range(4):
                            pieces_ahead(s, j, PIECE_KIND[kind], follows)
                            if kind == "up" and j == 3:
                                f, c, at = what
                                pair = i * per + (at + k)
                                done = i * per + (at + k + NCHUNK * UPS * f + UPS * c)
                                dve.wait_ge(piece_used, s * 8 + 8)
                                dve.wait_ge(drained[0], e_ + 1)
                                dve.wait_ge(act_ready, done)
                                TT(part[:, :, :], silu_g[:, :, :], main[:, 2:4, 0:COLS],
                                   ALU.mult).then_inc(drained[1], 1)
                                dve.wait_ge(drained[1], o_ + 1)
                                hi = act_hi[:, bass.ds(pair * 2, 2), :]
                                ch.link(TS(hi, part[:, :, :], 1.0, None, ALU.mult))
                                TT(act_lo[:, bass.ds(pair * 2, 2), :], part[:, :, :], hi.bitcast(F32),
                                   ALU.subtract).then_inc(act_ready, 1)
                            if kind == "down" and j == 3:
                                n0 = i * (2 * per) + 2 * (what[2] + k)
                                add_branch(s * 8 + 8, par, (e_, o_)[par], n0, squares)
                            if kind not in ("up", "down"):
                                dve_tasks(kind, what or 0, j, s, o_, e_)
                    if vec0 is not None:
                        mod_place(i + vec0)
                if kind == "down" and squares and (n + 1 == len(plan) or plan[n + 1][0] != "down"):
                    dve.memset(part2[:, 0, 0:1], 0.0).then_inc(sumsq_ready, 1)
                    if what[0] == 0:
                        lo_piece(S_XBC, 2, "full")
                        lo_piece(S_XBC, 3, "full")
                        make_gain(SC2, "g_mix")
                        norm(2, SH2, 17, KD, S_XBC, {})
            make_gain(SCF, "g_final")
            dve.wait_ge(std_ready, 5)
            ch.link(dve.reciprocal(rstd[:, :], rstd[:, :]))
            norm_samples()
            ysamp = part[:, 0, 0:P].rearrange("p (b k) -> p k b", k=KD)
            TT(ysamp, samp[:, :, :], mods[:, SHF, :, 1:9], ALU.add).then_inc(aff_ready, 1)

            def y_odd(q):
                dve.wait_ge(y_turned, q + 1)
                dve.tensor_copy(yrows[:, :, q * PAIR:(q + 1) * PAIR],
                                main[:, q % 4, :].rearrange("p (c n) -> p c n", c=2)).then_inc(y_rows_odd, 1)
            for k in range(KD):
                if k >= 4:
                    dve.wait_ge(y_turned, (k - 4) // 2 + 1)
                STT(ntile[:, k % 4, :], x[:, k, 0:NT], gain[:, k, 0:1], rstd[:, 0:NT],
                    ALU.mult, ALU.mult).then_inc(aff_ready, 1)
                if k % 4 == 2 and k >= 6:
                    y_odd(k // 2 - 2)
            y_odd(7)

        @block.tensor
        def _(pe):
            MM = nc.tensor.matmul

            def turn(out, src):
                return nc.tensor.transpose(out, src, ident[:, :])

            def turn_part(out, src, rows=P):
                return MM(out, src, ident[0:rows, 0:rows], start=True, stop=True)

            def ada_product(vec, k, first=False):
                if first:
                    src = (ada, ada_more)[(k // 2) % 2]
                    pe.wait_ge(first_landed[k % 4], 16 * (vec * 4 + k // 4 + 1))
                else:
                    src = ada
                    pe.wait_ge(ada_landed[k % 2], (vec - 2) * (8 * 16) + 16 * (k // 2 + 1))
                if k == 0:
                    if isinstance(vec, int) and vec == 0:
                        pe.wait_ge(c_ready, 1)
                    else:
                        pe.wait_ge(mod_ready, vec)
                for j in range(4):
                    last = MM(b4[32 * j:32 * j + 32, :], cT[:, k, :], src[:, k % 2, j * 512:(j + 1) * 512],
                              start=k == 0, stop=k == KD - 1, tile_position=(0, 32 * j))
                last.then_inc(ada_used, 1)

            def ada_turn(vec):
                pe.wait_ge(ada_copied, vec + 1)
                for q in range(4):
                    last = turn(b4[:, q * P:(q + 1) * P], ada_sum[:, q * P:(q + 1) * P])
                last.then_inc(ada_turned, 1)

            def sumsq_total(n):
                pe.wait_ge(sumsq_ready, n)
                MM(b6[:, 0:COLS], ones[:, :], sumsq[:, 0, :], start=True, stop=False)
                MM(b6[:, 0:COLS], ones[:, :], sumsq[:, 1, :], start=False, stop=True).then_inc(sumsq_spread, 1)

            def piece(s, m, kind, par, h_base=None, act_base=None, before=None, in_act=False):
                pe.wait_ge(lo_done, s * 8 + (m + 1))
                if before is not None and not (isinstance(before, int) and before == 0):
                    pe.wait_ge(drained[par], before)
                wide = WIDE[kind]
                group = PIECES[kind] if kind != "full" else PIECES[kind][4 * (m // 4):4 * (m // 4) + 4]
                at = sum(group[:m % 4 if kind == "full" else m])
                total = sum(group)
                for kk in range(PIECES[kind][m]):
                    k = at + kk
                    if h_base is not None:
                        pe.wait_ge(h_ready, h_base + k + 1)
                    if act_base is not None and (k % 2 == 0 or kk == 0):
                        pe.wait_ge(act_ready, act_base + k // 2 + 1)
                    hi, lo = (act_hi, act_lo) if in_act else (h_hi, h_lo)
                    for half in range(wide // P):
                        cols = slice(kk * wide + half * P, kk * wide + half * P + P)
                        out = main[:, 2 * par + half, 0:COLS]
                        wh, wl = w_hi[:, m % 4, cols], w_lo[:, m % 4, cols]
                        MM(out, wh, hi[:, k, :], start=k == 0, stop=False)
                        MM(out, wh, lo[:, k, :], start=False, stop=False)
                        last = MM(out, wl, hi[:, k, :], start=False, stop=k == total - 1)
                last.then_inc(piece_used, 1)

            def rows_batch(b):
                bank = (b5, b6)[b % 2]
                if b >= 2:
                    pe.wait_ge(rows_placed, b - 1)
                if b == 0:
                    pe.wait_ge(consts_ready, 1)
                    pe.wait_ge(c_rows, 16 * len([c for c in ROW_COPIES if c[2] < C_TILES]))
                    for tile in range(C_TILES):
                        last = turn(bank[:, tile * P:(tile + 1) * P], rowbuf[:, tile, :])
                elif b > KD // 2:
                    b -= KD // 2
                    pe.wait_ge(other_rows, OTHER_ROWS)
                    for n, tile in enumerate(range(C_TILES + 4 * (b - 1), min(C_TILES + 4 * b, ROW_TILES))):
                        rows = min(P, ROWS - tile * P)
                        last = (turn if rows == P else turn_part)(
                            bank[:, n * P:n * P + rows], rowbuf[0:rows, tile, :], *([rows] if rows < P else []))
                else:
                    pe.wait_ge(x_rows, 32)
                    k = 2 * (b - 1)
                    for kk in range(2):
                        for c in range(2):
                            last = turn(bank[:, kk * NT + c * P:kk * NT + (c + 1) * P],
                                        xrows[:, c, (k + kk) * P:(k + kk + 1) * P])
                last.then_inc(rows_turned, 1)

            rows_batch(0)
            batches = 1 + N_ROWB + KD // 2
            for k in range(KD):
                ada_product(SH1, k, first=True)
                if 2 <= k < 2 + batches - 1:
                    rows_batch(k - 1)
                if k == 2 + batches - 1:
                    MM(b7[:, 0:3 * NHEAD], ones[0:1, :], heads_row[0:1, :], start=True, stop=True).then_inc(heads_spread, 1)
            ada_turn(SH1)
            for k in range(KD):
                ada_product(SC1, k, first=True)
            sumsq_total(1)
            ada_turn(SC1)

            def prep(c):
                cs = slice(c * P, (c + 1) * P)
                if c == 0:
                    pe.wait_ge(xbc_ready, 6)
                    pe.wait_ge(samp_placed, 1)
                else:
                    pe.wait_ge(y_placed, 8)
                    pe.wait_ge(gate_taken, 12)
                for g in range(2):
                    turn(b4[:, g * P:(g + 1) * P], xbc[:, 8 + g, cs])
                    MM(b4[:, (2 + g) * P:(3 + g) * P], xbc[:, 8 + g, cs], xbc[:, 10 + g, cs], start=True, stop=True)
                for t in range(KW):
                    last = turn((b5, b6)[t // 4][:, (t % 4) * P:(t % 4 + 1) * P], xbc[:, t, cs])
                last.then_inc(prep_turned, 1)

            def states(c):
                pe.wait_ge(prep_done, c + 1)
                pe.wait_ge(st_placed, 2 + 2 * c)
                for t in range(KW):
                    last = MM((b5, b6)[t // 4][:, (t % 4) * P:(t % 4 + 1) * P], xdec[:, t * P:(t + 1) * P],
                              btok[:, t // 4, :], start=True, stop=True)
                last.then_inc(st_made, 1)

            def states_turned():
                pe.wait_ge(prep_done, 1)
                for g in range(2):
                    last = MM((b5, b6)[g][:, :], btok[:, g, :], xdec[:, g * 512:(g + 1) * 512], start=True, stop=True)
                last.then_inc(st_made, 1)

            def bcast(k):
                c, t = k // 8, k % 8
                if k == 0:
                    pe.wait_ge(st_placed, 4)
                else:
                    pe.wait_ge(d_ready, k)
                if k == 8:
                    pe.wait_ge(prep_done, 3)
                if k > 8:
                    pe.wait_ge(cexp_raw, k - 8)
                for j in range(2):
                    h = 2 * t + j
                    last = MM(b5[:, j * P:(j + 1) * P], dA[:, c, h:h + 1].to_broadcast([P, P]), tri[:, :],
                              start=True, stop=True)
                last.then_inc(bc_made, 1)

            def y_item(k):
                c, t = k // 8, k % 8
                pe.wait_ge(m_ready, k + 1)
                if k:
                    pe.wait_ge(y_placed, k)
                for j in range(2):
                    h = 2 * t + j
                    last = MM(b6[64 * j:64 * j + 64, 0:P], xdt[:, 64 * h:64 * h + 64], dmat[:, k % 2, j, :],
                              start=True, stop=c == 0)
                for j in range(2 * c):
                    h = 2 * t + j
                    last = MM(b6[64 * j:64 * j + 64, 0:P], s0t[:, 64 * h:64 * h + 64], cexp[:, j, :],
                              start=False, stop=True)
                last.then_inc(y_made, 1)

            def diag_sum(n):
                pe.wait_ge(diag_ready, n + 1)
                if n:
                    pe.wait_ge(spread_done, n)
                if n % 2 == 0 and n:
                    pe.wait_ge(gate_taken, 2 * n)
                MM(b7[:, :], ones[:, :], diag.rearrange("p b n -> p (b n)"), start=True, stop=True).then_inc(diag_spread, 1)

            def gates(t):
                pe.wait_ge(gates_in, 64)
                pe.wait_ge(conv_ready, 12 + 2 * (t // 2) + 2)
                if t:
                    pe.wait_ge(gate_taken, 2 * t)
                if t % 2 == 0:
                    pe.wait_ge(spread_done, t + 2)
                if t == 0:
                    pe.wait_ge(prep_done, 1)
                if t == 6:
                    pe.wait_ge(prep_done, 2)
                MM(b4[:, 0:COLS], gates_w[:, 0, t, :], cval[:, t % 2, :], start=True, stop=True)
                MM(b7[:, 0:COLS], gates_w[:, 1, t, :], cval[:, t % 2, :], start=True, stop=True).then_inc(gate_made, 1)

            def pe_tasks(kind, t, j, e_):
                u = 4 * t + j
                if kind == "xbc":
                    if u == 4:
                        pe.wait_ge(drained[0], E_DT + 1)
                        pe.wait_ge(std_ready, 2)
                        turn(b6[:, 0:P], dtq[:, 0:P])
                        turn(b6[:, P:2 * P], dtq[:, P:2 * P])
                        turn_part(b6[0:NB, 2 * P:3 * P], dtq[:, 2 * P:2 * P + NB]).then_inc(dt_turned, 1)
                    if u == 7:
                        pe.wait_ge(dA_ready, 1)
                        both = dA[:, 0:2, :].rearrange("p c h -> p (c h)")
                        MM(b7[:, 0:32], tri[:, :], both, start=True, stop=True)
                        MM(b7[:, 32:64], ones[:, :], both, start=True, stop=True).then_inc(cs_spread, 1)
                    if u == 10:
                        pe.wait_ge(dexp_ready, 1)
                        MM(b6[:, 0:2 * P].rearrange("p (a n) -> p a n", a=2), ones[0:NB, :],
                           sumsq[0:NB, :, 0:P], start=True, stop=True).then_inc(samp_spread, 1)
                if kind in ("lru", "z"):
                    r = u + (16 if kind == "z" else 0)
                    if r == 0:
                        prep(0)
                    if r == 2:
                        states_turned()
                    if r == 3:
                        states(0)
                    if 5 <= r <= 12:
                        y_item(r - 5)
                    if 16 <= r <= 23:
                        y_item(r - 8)
                    if 4 <= r <= 11:
                        bcast(r - 4)
                    if r == 13:
                        prep(1)
                    if r == 14:
                        states(1)
                    if 15 <= r <= 22:
                        bcast(r - 7)
                if kind == "lru":
                    if j < 2:
                        diag_sum(2 * t + j)
                    else:
                        gates(2 * t + j - 2)
                if kind == "out" and u == 1:
                    pe.wait_ge(captured, 10)
                    pe.wait_ge(h_captured, 4)
                    for tile in range(OUT_TILES):
                        bank = (b5, b6)[tile // 4]
                        if tile == 4:
                            pe.wait_ge(std_ready, 3)
                        last = turn(bank[:, (tile % 4) * P:(tile % 4 + 1) * P], outcol[:, tile * P:(tile + 1) * P])
                        if tile == 3 or tile == OUT_TILES - 1:
                            last.then_inc(out_turned, 1)
                if kind == "out" and u == 15:
                    pe.wait_ge(out_rows_ready, 1)
                    sumsq_total(4)

            for n, seg in enumerate(plan):
                kind, s_first, count, per, vec0, _, _, what = seg
                pk = PIECE_KIND[kind]
                h_base, act_base = None, None
                if kind == "up" and what[1:] == (0, 0):
                    h_base = (0, 3 * KD)[what[0]]
                if kind == "xbc" and what == 0:
                    h_base = KD
                if kind == "out" and what == 0:
                    h_base = 2 * KD
                if kind == "down" and what[2] == 0:
                    act_base = NCHUNK * UPS * what[0] + UPS * what[1]
                for i, last in turns(pe, seg, peel_first=n == 0):
                    for k in range(per):
                        s, e_, o_, par = at_step(seg, i, k)
                        for j in range(4):
                            if vec0 is not None:
                                ada_product(i + vec0, 4 * k + j)
                            for m in (2 * j, 2 * j + 1):
                                if kind == "out" and what == 0 and m == 1:
                                    pe.wait_ge(y_placed, 16)
                                    sumsq_total(3)
                                if pk == "full":
                                    par_m, first = m // 4, m % 4 == 0
                                else:
                                    par_m, first = par, m == 0
                                piece(s, m, pk, par_m, h_base if m < 4 else None,
                                      act_base, (e_, o_)[par_m] if first else None, kind == "down")
                            if kind not in ("up", "down"):
                                pe_tasks(kind, what or 0, j, e_)
                    if vec0 is not None:
                        ada_turn(i + vec0)
                if kind == "down" and what[1] == NCHUNK - 1 and (n + 1 == len(plan) or plan[n + 1][0] != "down"):
                    sumsq_total(2 if what[0] == 0 else 5)

            for q in range(KW):
                pe.wait_ge(hhi_ready, HHI_FINAL + 2 * q + 2)
                if q >= 4:
                    pe.wait_ge((y_rows_even, y_rows_odd)[q % 2], (q - 4) // 2 + 1)
                for kk in range(2):
                    for c in range(2):
                        last = turn(main[:, q % 4, c * NT + kk * P:c * NT + (kk + 1) * P],
                                    ntile[:, (2 * q + kk) % 4, c * P:(c + 1) * P])
                last.then_inc(y_turned, 1)
            turn(b7[:, 0:P], part[:, 0, 0:P]).then_inc(y_turned, 1)


_INS = ["x_prompt", "x_sample", "c_prompt", "c_sample", "state_lru_h", "state_lru_conv", "state_ssm",
        "state_ssd_conv", "w_ada", "b_ada", "g_ffn1", "w_up1", "w_down1", "g_mix", "w_in", "lru_conv_w",
        "lru_conv_b", "lru_wa", "lru_ba", "lru_wi", "lru_bi", "lru_lambda", "ssd_conv_w", "ssd_conv_b",
        "ssd_dt_bias", "ssd_A_log", "ssd_D", "ssd_norm_g", "w_out", "g_ffn2", "w_up2", "w_down2",
        "w_ada_f", "b_ada_f", "g_final"]
_OUTS = [("y_prompt", (1, NT, D)), ("y_sample", (NB, 1, D)), ("lru_h_prompt", (1, 1, W)),
         ("lru_conv_prompt", (1, 1, CW - 1, W)), ("ssm_prompt", (1, 1, NHEAD, 64, NSTATE)),
         ("ssd_conv_prompt", (1, 1, CW - 1, CONV_C)), ("lru_h_sample", (1, NB, W)),
         ("lru_conv_sample", (1, NB, CW - 1, W)), ("ssm_sample", (1, NB, NHEAD, 64, NSTATE)),
         ("ssd_conv_sample", (1, NB, CW - 1, CONV_C))]


def kernel(**inputs):
    import numpy as _np
    import concourse.bacc as _bacc
    from concourse import mybir as _mybir
    from concourse.bass_utils import run_bass_kernel_spmd as _run

    nc = _bacc.Bacc("TRN2", target_bir_lowering=False, num_devices=1, dynamic_dma_scratch_size=1024)
    arrays, ins, outs = {}, {}, {}
    for name in _INS:
        a = _np.ascontiguousarray(inputs[name])
        arrays[f"in_{name}"] = a
        ins[name] = nc.dram_tensor(f"in_{name}", a.shape, _mybir.dt.from_np(a.dtype), kind="ExternalInput").ap()
    for name, shape in _OUTS:
        outs[name] = nc.dram_tensor(f"out_{name}", shape, _mybir.dt.float32, kind="ExternalOutput").ap()
    build(nc, ins, outs)
    r = _run(nc, [arrays], core_ids=[0])
    return tuple(r.results[0][f"out_{name}"] for name, _ in _OUTS)
```
